# Optimizing a Trainium2 kernel written in Bass

```python
import math
import jax, jax.numpy as jnp
from jax import lax
import numpy as np

D_MODEL = 1024
BATCH = 1
SEQ = 512
DEPTH = 2

N_A = DEPTH // 2
N_B = DEPTH - N_A
HEAD_DIM = 64
MIX_WIDTH = D_MODEL
MEM_HEADS = 4
MEM_WIDTH = MEM_HEADS * HEAD_DIM
MEM_LEN = 256
CONV_CH = MIX_WIDTH - MEM_WIDTH
CONV_K = 3
NSA_HEADS = CONV_CH // HEAD_DIM
NSA_KV_GROUPS = 2
NSA_HPG = NSA_HEADS // NSA_KV_GROUPS
N_BRANCH = 3
NSA_Q_WIDTH = NSA_HEADS * HEAD_DIM
NSA_GATE_WIDTH = NSA_HEADS * N_BRANCH
CMP_LEN = 32
CMP_STRIDE = 16
CMP_HIDDEN = 256
SEL_BLOCK = 64
SEL_TOPK = 16
N_LOCAL_SEL = 2
WINDOW = 512
Q_BLOCK = 128
REL_BUCKETS = 32
REL_MAX_DIST = 1024
FF_DIM = 4 * D_MODEL
EPS = 1e-6
NEG = -1e30
FORCE_SCORE = 1e4


def rmsnorm(x, g):
    xf = x.astype(jnp.float32)
    y = xf * lax.rsqrt(jnp.mean(xf * xf, axis=-1, keepdims=True) + EPS)
    return (y * g.astype(jnp.float32)).astype(x.dtype)

def rel_bucket(dist):
    n = jnp.maximum(dist, 0)
    max_exact = REL_BUCKETS // 2
    nf = jnp.maximum(n, 1).astype(jnp.float32)
    large = max_exact + (jnp.log(nf / max_exact) / math.log(REL_MAX_DIST / max_exact)
                         * (REL_BUCKETS - max_exact)).astype(jnp.int32)
    large = jnp.minimum(large, REL_BUCKETS - 1)
    return jnp.where(n < max_exact, n, large)

def masked_softmax(logits, mask):
    p = jax.nn.softmax(jnp.where(mask, logits, NEG), axis=-1)
    return jnp.where(mask, p, 0.0)

def selection_overlap(n_cmp, n_sel):
    c0 = np.arange(n_cmp)[:, None] * CMP_STRIDE
    s0 = np.arange(n_sel)[None, :] * SEL_BLOCK
    ov = np.minimum(c0 + CMP_LEN, s0 + SEL_BLOCK) - np.maximum(c0, s0)
    return np.clip(ov, 0, None).astype(np.float32) / CMP_LEN

def short_conv_mixer(z, conv_w):
    gate_b, gate_c, u = jnp.split(z, 3, axis=-1)
    v = gate_c * u
    y = lax.conv_general_dilated(
        v, conv_w[:, None, :].astype(v.dtype), window_strides=(1,),
        padding=[(CONV_K - 1, 0)], dimension_numbers=('NWC', 'WIO', 'NWC'),
        feature_group_count=CONV_CH)
    return gate_b * y

def memory_attention(q_raw, mem_k, mem_v, q_gain):
    b, s, _ = q_raw.shape
    q = rmsnorm(q_raw.reshape(b, s, MEM_HEADS, HEAD_DIM), q_gain) * (HEAD_DIM ** -0.5)
    lg = jnp.einsum('bshd,bmhd->bhsm', q, mem_k).astype(jnp.float32)
    p = jax.nn.softmax(lg, axis=-1).astype(mem_v.dtype)
    return jnp.einsum('bhsm,bmhd->bshd', p, mem_v).reshape(b, s, MEM_WIDTH)

def compress(u, pos, w1, w2):
    b, s, g, d = u.shape
    ch = u.reshape(b, s // CMP_STRIDE, CMP_STRIDE, g, d)
    blk = jnp.concatenate([ch[:, :-1], ch[:, 1:]], axis=2) + pos[:, None, :]
    flat = blk.transpose(0, 1, 3, 2, 4).reshape(b, -1, g, CMP_LEN * d)
    return jax.nn.gelu(flat @ w1) @ w2

def build_shared_kv(x, kv_norm, w_kv_shared, k_gain, cmp_pos, cmp_w1, cmp_w2):
    b, s, _ = x.shape
    h = rmsnorm(x, kv_norm)
    kv = (h @ w_kv_shared).reshape(b, s, 6, NSA_KV_GROUPS, HEAD_DIM)
    kc = rmsnorm(compress(kv[:, :, 0], cmp_pos[0], cmp_w1[0], cmp_w2[0]), k_gain[0])
    vc = compress(kv[:, :, 1], cmp_pos[1], cmp_w1[1], cmp_w2[1])
    n_sel = s // SEL_BLOCK
    def to_blocks(u):
        return u.reshape(b, n_sel, SEL_BLOCK, NSA_KV_GROUPS, HEAD_DIM).transpose(0, 3, 1, 2, 4)
    ks = to_blocks(rmsnorm(kv[:, :, 2], k_gain[1]))
    vs = to_blocks(kv[:, :, 3])
    def pad_front(u):
        return jnp.pad(u, ((0, 0), (WINDOW, 0), (0, 0), (0, 0)))
    kw = pad_front(rmsnorm(kv[:, :, 4], k_gain[2]))
    vw = pad_front(kv[:, :, 5])
    return (kc, vc, ks, vs, kw, vw)

def nsa_mixer(q_raw, gate_logits, q_gain, kc, vc, ks, vs, kw, vw, rel_bias):
    b, s, _ = q_raw.shape
    G, Hg, hd = NSA_KV_GROUPS, NSA_HPG, HEAD_DIM
    q = rmsnorm(q_raw.reshape(b, s, G, Hg, hd), q_gain) * (hd ** -0.5)
    gates = jax.nn.sigmoid(gate_logits.reshape(b, s, G, Hg, N_BRANCH))
    n_cmp = kc.shape[1]
    n_sel = ks.shape[2]
    topk = min(SEL_TOPK, n_sel)
    overlap = jnp.asarray(selection_overlap(n_cmp, n_sel), dtype=jnp.float32)
    cmp_end = jnp.arange(n_cmp) * CMP_STRIDE + CMP_LEN - 1
    sel_idx = jnp.arange(n_sel)
    table = rel_bias.astype(jnp.float32)
    table_g = table.reshape(REL_BUCKETS, G, Hg).transpose(1, 0, 2)
    bi = jnp.arange(b)[:, None, None, None]
    gi = jnp.arange(G)[None, :, None, None]
    kw_len = WINDOW + Q_BLOCK

    def block(i):
        s0 = i * Q_BLOCK
        tq = s0 + jnp.arange(Q_BLOCK)
        qb = lax.dynamic_slice_in_dim(q, s0, Q_BLOCK, axis=1)
        gb = lax.dynamic_slice_in_dim(gates, s0, Q_BLOCK, axis=1)
        d_c = tq[:, None] - cmp_end[None, :]
        bias_c = table[rel_bucket(d_c)].reshape(Q_BLOCK, n_cmp, G, Hg).transpose(2, 3, 0, 1)
        lg = jnp.einsum('bqghd,bcgd->bghqc', qb, kc).astype(jnp.float32) + bias_c
        p_c = masked_softmax(lg, d_c >= 0)
        o_c = jnp.einsum('bghqc,bcgd->bqghd', p_c.astype(vc.dtype), vc)
        imp = jnp.einsum('bghqc,cj->bgqj', p_c, overlap)
        back = (tq // SEL_BLOCK)[:, None] - sel_idx[None, :]
        forced = (sel_idx[None, :] == 0) | ((back >= 0) & (back < N_LOCAL_SEL))
        score = jnp.where(back >= 0, jnp.where(forced, FORCE_SCORE, imp), NEG)
        _, idx = lax.top_k(score, topk)
        k_sel = ks[bi, gi, idx].reshape(b, G, Q_BLOCK, topk * SEL_BLOCK, hd)
        v_sel = vs[bi, gi, idx].reshape(b, G, Q_BLOCK, topk * SEL_BLOCK, hd)
        pos_s = (idx[..., None] * SEL_BLOCK + jnp.arange(SEL_BLOCK)).reshape(b, G, Q_BLOCK, topk * SEL_BLOCK)
        d_s = tq[None, None, :, None] - pos_s
        bias_s = table_g[gi, rel_bucket(d_s)].transpose(0, 1, 4, 2, 3)
        lg = jnp.einsum('bqghd,bgqkd->bghqk', qb, k_sel).astype(jnp.float32) + bias_s
        p_s = masked_softmax(lg, (d_s >= 0)[:, :, None])
        o_s = jnp.einsum('bghqk,bgqkd->bqghd', p_s.astype(v_sel.dtype), v_sel)
        k_w = lax.dynamic_slice_in_dim(kw, s0, kw_len, axis=1)
        v_w = lax.dynamic_slice_in_dim(vw, s0, kw_len, axis=1)
        pos_w = s0 - WINDOW + jnp.arange(kw_len)
        d_w = tq[:, None] - pos_w[None, :]
        mask_w = (d_w >= 0) & (d_w < WINDOW) & (pos_w[None, :] >= 0)
        bias_w = table[rel_bucket(d_w)].reshape(Q_BLOCK, kw_len, G, Hg).transpose(2, 3, 0, 1)
        lg = jnp.einsum('bqghd,bkgd->bghqk', qb, k_w).astype(jnp.float32) + bias_w
        p_w = masked_softmax(lg, mask_w)
        o_w = jnp.einsum('bghqk,bkgd->bqghd', p_w.astype(v_w.dtype), v_w)
        return gb[..., 0:1] * o_c + gb[..., 1:2] * o_s + gb[..., 2:3] * o_w

    out = lax.map(block, jnp.arange(s // Q_BLOCK))
    return jnp.moveaxis(out, 0, 1).reshape(b, s, NSA_Q_WIDTH)

def first_inputs(seed: int = 0) -> dict:
    key = jax.random.key(seed)
    ks = jax.random.split(key, 22)
    def nrm(k, shape, scale):
        return jax.random.normal(k, shape, jnp.float32) * scale
    def gain(k, shape):
        return 1.0 + 0.1 * jax.random.normal(k, shape, jnp.float32)
    a_in = 3 * CONV_CH + MEM_WIDTH
    b_in = NSA_Q_WIDTH + NSA_GATE_WIDTH + MEM_WIDTH
    return {
        "x": nrm(ks[0], (BATCH, SEQ, D_MODEL), 1.0),
        "mem": nrm(ks[1], (BATCH, MEM_LEN, D_MODEL), 1.0),
        "mix_norm": gain(ks[2], (DEPTH, D_MODEL)),
        "a_w_in": nrm(ks[3], (N_A, D_MODEL, a_in), D_MODEL ** -0.5),
        "a_conv_w": nrm(ks[4], (N_A, CONV_K, CONV_CH), CONV_K ** -0.5),
        "b_w_in": nrm(ks[5], (N_B, D_MODEL, b_in), D_MODEL ** -0.5),
        "b_q_gain": gain(ks[6], (N_B, HEAD_DIM)),
        "kv_norm": gain(ks[7], (D_MODEL,)),
        "w_kv_shared": nrm(ks[8], (D_MODEL, 6 * NSA_KV_GROUPS * HEAD_DIM), D_MODEL ** -0.5),
        "k_gain": gain(ks[9], (N_BRANCH, HEAD_DIM)),
        "cmp_pos": nrm(ks[10], (2, CMP_LEN, HEAD_DIM), 0.1),
        "cmp_w1": nrm(ks[11], (2, CMP_LEN * HEAD_DIM, CMP_HIDDEN), (CMP_LEN * HEAD_DIM) ** -0.5),
        "cmp_w2": nrm(ks[12], (2, CMP_HIDDEN, HEAD_DIM), CMP_HIDDEN ** -0.5),
        "rel_bias": nrm(ks[13], (REL_BUCKETS, NSA_HEADS), 0.5),
        "mem_norm": gain(ks[14], (D_MODEL,)),
        "mem_w_kv": nrm(ks[15], (DEPTH, D_MODEL, 2 * MEM_WIDTH), D_MODEL ** -0.5),
        "mem_q_gain": gain(ks[16], (DEPTH, HEAD_DIM)),
        "mem_k_gain": gain(ks[17], (DEPTH, HEAD_DIM)),
        "w_out": nrm(ks[18], (DEPTH, MIX_WIDTH, D_MODEL), MIX_WIDTH ** -0.5),
        "mlp_norm": gain(ks[19], (DEPTH, D_MODEL)),
        "w_up": nrm(ks[20], (DEPTH, D_MODEL, FF_DIM), D_MODEL ** -0.5),
        "w_down": nrm(ks[21], (DEPTH, FF_DIM, D_MODEL), FF_DIM ** -0.5),
    }

def first_block(x, mem, mix_norm, a_w_in, a_conv_w, b_w_in, b_q_gain, kv_norm, w_kv_shared,
              k_gain, cmp_pos, cmp_w1, cmp_w2, rel_bias, mem_norm, mem_w_kv, mem_q_gain,
              mem_k_gain, w_out, mlp_norm, w_up, w_down):
    b, m, _ = mem.shape
    mem_h = rmsnorm(mem, mem_norm)
    shared = None
    for layer in range(DEPTH):
        h = rmsnorm(x, mix_norm[layer])
        mkv = (mem_h @ mem_w_kv[layer]).reshape(b, m, 2, MEM_HEADS, HEAD_DIM)
        mem_k = rmsnorm(mkv[:, :, 0], mem_k_gain[layer])
        mem_v = mkv[:, :, 1]
        if layer < N_A:
            z = h @ a_w_in[layer]
            y_tok = short_conv_mixer(z[..., :3 * CONV_CH], a_conv_w[layer])
            q_mem = z[..., 3 * CONV_CH:]
        else:
            j = layer - N_A
            z = h @ b_w_in[j]
            y_tok = nsa_mixer(z[..., :NSA_Q_WIDTH],
                              z[..., NSA_Q_WIDTH:NSA_Q_WIDTH + NSA_GATE_WIDTH],
                              b_q_gain[j], *shared, rel_bias)
            q_mem = z[..., NSA_Q_WIDTH + NSA_GATE_WIDTH:]
        y_mem = memory_attention(q_mem, mem_k, mem_v, mem_q_gain[layer])
        x = x + jnp.concatenate([y_tok, y_mem], axis=-1) @ w_out[layer]
        hm = rmsnorm(x, mlp_norm[layer])
        x = x + jnp.square(jax.nn.relu(hm @ w_up[layer])) @ w_down[layer]
        if layer == N_A - 1:
            shared = build_shared_kv(x, kv_norm, w_kv_shared, k_gain, cmp_pos, cmp_w1, cmp_w2)
    return x


N_MIXERS = 2
N_MLA_LAYERS = (DEPTH + 1) // 2
N_DIFF_LAYERS = DEPTH // 2

MLA_NOPE = 128
MLA_ROPE = 64
MLA_V = 128
MLA_HEADS = D_MODEL // MLA_V
MLA_Q_LORA = 384
MLA_KV_LORA = 256
MLA_ROPE_THETA = 10000.0

DIFF_HEAD_DIM = 64
DIFF_HEADS = D_MODEL // (2 * DIFF_HEAD_DIM)
DIFF_ROT_DIM = DIFF_HEAD_DIM // 4
ROPE_THETA = 500000.0

D_FF = 4 * D_MODEL
DEEPNORM_ALPHA = (2 * DEPTH) ** 0.25
DEEPNORM_BETA = (8 * DEPTH) ** -0.25
LN_EPS = 1e-5
RMS_EPS = 1e-6


def _layernorm(x, g, b):
    xf = x.astype(jnp.float32)
    mu = jnp.mean(xf, axis=-1, keepdims=True)
    var = jnp.mean(jnp.square(xf - mu), axis=-1, keepdims=True)
    y = (xf - mu) * lax.rsqrt(var + LN_EPS) * g.astype(jnp.float32) + b.astype(jnp.float32)
    return y.astype(x.dtype)

def _rmsnorm(x, g):
    xf = x.astype(jnp.float32)
    y = xf * lax.rsqrt(jnp.mean(jnp.square(xf), axis=-1, keepdims=True) + RMS_EPS)
    return (y * g.astype(jnp.float32)).astype(x.dtype)

def _rope(x, positions, theta):
    d = x.shape[-1]
    inv_freq = theta ** (-jnp.arange(0, d, 2, dtype=jnp.float32) / d)
    ang = positions.astype(jnp.float32)[:, :, None] * inv_freq
    cos = jnp.cos(ang)[:, :, None, :]
    sin = jnp.sin(ang)[:, :, None, :]
    xf = x.astype(jnp.float32)
    x1, x2 = xf[..., : d // 2], xf[..., d // 2:]
    out = jnp.concatenate([x1 * cos - x2 * sin, x2 * cos + x1 * sin], axis=-1)
    return out.astype(x.dtype)

def _partial_rope(x, positions, rot_dim, theta):
    return jnp.concatenate([_rope(x[..., :rot_dim], positions, theta), x[..., rot_dim:]], axis=-1)

def _to_blocks(t):
    b, s = t.shape[0], t.shape[1]
    return t.reshape(b, s // Q_BLOCK, Q_BLOCK, *t.shape[2:]).swapaxes(0, 1)

def _from_blocks(t):
    n, b, qb = t.shape[0], t.shape[1], t.shape[2]
    return t.swapaxes(0, 1).reshape(b, n * qb, *t.shape[3:])

def _causal_probs(q_blk, k, q_start, scale):
    s = jnp.einsum('bqhd,bkhd->bhqk', q_blk, k).astype(jnp.float32) * scale
    q_idx = q_start + jnp.arange(q_blk.shape[1])
    k_idx = jnp.arange(k.shape[1])
    s = jnp.where(k_idx[None, :] <= q_idx[:, None], s, -jnp.inf)
    return jax.nn.softmax(s, axis=-1)

def _mla(x, positions, w_dq, q_norm, w_uq, w_dkv, kv_norm, w_ukv, w_o):
    b, s, _ = x.shape
    h = MLA_HEADS
    cq = _rmsnorm(x @ w_dq, q_norm)
    q = (cq @ w_uq).reshape(b, s, h, MLA_NOPE + MLA_ROPE)
    q = jnp.concatenate([q[..., :MLA_NOPE], _rope(q[..., MLA_NOPE:], positions, MLA_ROPE_THETA)], axis=-1)
    ckv = x @ w_dkv
    c_kv = _rmsnorm(ckv[..., :MLA_KV_LORA], kv_norm)
    k_pe = _rope(ckv[..., None, MLA_KV_LORA:], positions, MLA_ROPE_THETA)
    kv = (c_kv @ w_ukv).reshape(b, s, h, MLA_NOPE + MLA_V)
    k = jnp.concatenate([kv[..., :MLA_NOPE], jnp.broadcast_to(k_pe, (b, s, h, MLA_ROPE))], axis=-1)
    v = kv[..., MLA_NOPE:]
    scale = (MLA_NOPE + MLA_ROPE) ** -0.5
    starts = jnp.arange(s // Q_BLOCK) * Q_BLOCK

    def block(args):
        q_blk, start = args
        p = _causal_probs(q_blk, k, start, scale)
        return jnp.einsum('bhqk,bkhd->bqhd', p.astype(v.dtype), v)

    o = _from_blocks(lax.map(block, (_to_blocks(q), starts)))
    return o.reshape(b, s, h * MLA_V) @ w_o

def _diff_attn(x, positions, w_qkv, lq1, lk1, lq2, lk2, subln, w_o, lambda_init):
    b, s, _ = x.shape
    h, dh = DIFF_HEADS, DIFF_HEAD_DIM
    q, k, v = jnp.split(x @ w_qkv, 3, axis=-1)
    q = _partial_rope(q.reshape(b, s, 2 * h, dh), positions, DIFF_ROT_DIM, ROPE_THETA).reshape(b, s, h, 2, dh)
    k = _partial_rope(k.reshape(b, s, 2 * h, dh), positions, DIFF_ROT_DIM, ROPE_THETA).reshape(b, s, h, 2, dh)
    v = v.reshape(b, s, h, 2 * dh)
    k1, k2 = k[..., 0, :], k[..., 1, :]
    lam = (jnp.exp(jnp.sum(lq1.astype(jnp.float32) * lk1.astype(jnp.float32)))
           - jnp.exp(jnp.sum(lq2.astype(jnp.float32) * lk2.astype(jnp.float32)))
           + lambda_init)
    scale = dh ** -0.5
    starts = jnp.arange(s // Q_BLOCK) * Q_BLOCK

    def block(args):
        q_blk, start = args
        p1 = _causal_probs(q_blk[..., 0, :], k1, start, scale)
        p2 = _causal_probs(q_blk[..., 1, :], k2, start, scale)
        a = p1 - lam * p2
        return jnp.einsum('bhqk,bkhd->bqhd', a.astype(v.dtype), v)

    o = _from_blocks(lax.map(block, (_to_blocks(q), starts)))
    o = _rmsnorm(o, subln) * (1.0 - lambda_init)
    return o.reshape(b, s, h * 2 * dh) @ w_o

def _sqrelu_mlp(x, w_up, w_down):
    return jnp.square(jax.nn.relu(x @ w_up)) @ w_down

def second_inputs(seed: int = 0) -> dict:
    key = jax.random.key(seed)
    ks = jax.random.split(key, 24)
    f32 = jnp.float32
    nrm = lambda k, shape, scale: jax.random.normal(k, shape, f32) * scale
    na, nd, L = N_MLA_LAYERS, N_DIFF_LAYERS, DEPTH
    x = jax.random.normal(ks[0], (BATCH, SEQ, D_MODEL), f32)
    offsets = jax.random.randint(ks[1], (BATCH, 1), 0, 4096, dtype=jnp.int32)
    positions = (jnp.arange(SEQ, dtype=jnp.int32)[None, :] + offsets).astype(jnp.int32)
    return {
        "x": x,
        "positions": positions,
        "ln_mix_g": 1.0 + nrm(ks[2], (L, D_MODEL), 0.02),
        "ln_mix_b": nrm(ks[3], (L, D_MODEL), 0.02),
        "mla_w_dq": nrm(ks[4], (na, D_MODEL, MLA_Q_LORA), D_MODEL ** -0.5),
        "mla_q_norm": 1.0 + nrm(ks[5], (na, MLA_Q_LORA), 0.02),
        "mla_w_uq": nrm(ks[6], (na, MLA_Q_LORA, MLA_HEADS * (MLA_NOPE + MLA_ROPE)), MLA_Q_LORA ** -0.5),
        "mla_w_dkv": nrm(ks[7], (na, D_MODEL, MLA_KV_LORA + MLA_ROPE), D_MODEL ** -0.5),
        "mla_kv_norm": 1.0 + nrm(ks[8], (na, MLA_KV_LORA), 0.02),
        "mla_w_ukv": nrm(ks[9], (na, MLA_KV_LORA, MLA_HEADS * (MLA_NOPE + MLA_V)), MLA_KV_LORA ** -0.5),
        "mla_w_o": nrm(ks[10], (na, MLA_HEADS * MLA_V, D_MODEL), DEEPNORM_BETA * (MLA_HEADS * MLA_V) ** -0.5),
        "diff_w_qkv": nrm(ks[11], (nd, D_MODEL, 3 * DIFF_HEADS * 2 * DIFF_HEAD_DIM), D_MODEL ** -0.5),
        "diff_lambda_q1": nrm(ks[12], (nd, DIFF_HEAD_DIM), 0.1),
        "diff_lambda_k1": nrm(ks[13], (nd, DIFF_HEAD_DIM), 0.1),
        "diff_lambda_q2": nrm(ks[14], (nd, DIFF_HEAD_DIM), 0.1),
        "diff_lambda_k2": nrm(ks[15], (nd, DIFF_HEAD_DIM), 0.1),
        "diff_subln": 1.0 + nrm(ks[16], (nd, 2 * DIFF_HEAD_DIM), 0.02),
        "diff_w_o": nrm(ks[17], (nd, DIFF_HEADS * 2 * DIFF_HEAD_DIM, D_MODEL), DEEPNORM_BETA * D_MODEL ** -0.5),
        "ln_ffn_g": 1.0 + nrm(ks[18], (L, D_MODEL), 0.02),
        "ln_ffn_b": nrm(ks[19], (L, D_MODEL), 0.02),
        "ffn_w_up": nrm(ks[20], (L, D_MODEL, D_FF), D_MODEL ** -0.5),
        "ffn_w_down": nrm(ks[21], (L, D_FF, D_MODEL), DEEPNORM_BETA * D_FF ** -0.5),
    }

def second_block(x, positions, ln_mix_g, ln_mix_b, mla_w_dq, mla_q_norm, mla_w_uq, mla_w_dkv,
              mla_kv_norm, mla_w_ukv, mla_w_o, diff_w_qkv, diff_lambda_q1, diff_lambda_k1,
              diff_lambda_q2, diff_lambda_k2, diff_subln, diff_w_o, ln_ffn_g, ln_ffn_b,
              ffn_w_up, ffn_w_down):
    for i in range(DEPTH):
        j = i // N_MIXERS
        if i % N_MIXERS == 0:
            m = _mla(x, positions, mla_w_dq[j], mla_q_norm[j], mla_w_uq[j], mla_w_dkv[j],
                     mla_kv_norm[j], mla_w_ukv[j], mla_w_o[j])
        else:
            lambda_init = 0.8 - 0.6 * math.exp(-0.3 * i)
            m = _diff_attn(x, positions, diff_w_qkv[j], diff_lambda_q1[j], diff_lambda_k1[j],
                           diff_lambda_q2[j], diff_lambda_k2[j], diff_subln[j], diff_w_o[j],
                           lambda_init)
        x = _layernorm(DEEPNORM_ALPHA * x + m, ln_mix_g[i], ln_mix_b[i])
        x = _layernorm(DEEPNORM_ALPHA * x + _sqrelu_mlp(x, ffn_w_up[i], ffn_w_down[i]),
                       ln_ffn_g[i], ln_ffn_b[i])
    return x


def setup_inputs(seed=0):
    out = dict(first_inputs(seed))
    for name, value in second_inputs(seed + 1).items():
        if name != "x":
            out[name + "_2"] = value
    return out


def reference(
    x, mem, mix_norm, a_w_in, a_conv_w, b_w_in, b_q_gain, kv_norm, w_kv_shared, k_gain, cmp_pos,
    cmp_w1, cmp_w2, rel_bias, mem_norm, mem_w_kv, mem_q_gain, mem_k_gain, w_out, mlp_norm, w_up,
    w_down, positions_2, ln_mix_g_2, ln_mix_b_2, mla_w_dq_2, mla_q_norm_2, mla_w_uq_2,
    mla_w_dkv_2, mla_kv_norm_2, mla_w_ukv_2, mla_w_o_2, diff_w_qkv_2, diff_lambda_q1_2,
    diff_lambda_k1_2, diff_lambda_q2_2, diff_lambda_k2_2, diff_subln_2, diff_w_o_2, ln_ffn_g_2,
    ln_ffn_b_2, ffn_w_up_2, ffn_w_down_2,
):
    x = first_block(
        x, mem, mix_norm, a_w_in, a_conv_w, b_w_in, b_q_gain, kv_norm, w_kv_shared, k_gain,
        cmp_pos, cmp_w1, cmp_w2, rel_bias, mem_norm, mem_w_kv, mem_q_gain, mem_k_gain, w_out,
        mlp_norm, w_up, w_down,
    )
    return second_block(
        x, positions_2, ln_mix_g_2, ln_mix_b_2, mla_w_dq_2, mla_q_norm_2, mla_w_uq_2,
        mla_w_dkv_2, mla_kv_norm_2, mla_w_ukv_2, mla_w_o_2, diff_w_qkv_2, diff_lambda_q1_2,
        diff_lambda_k1_2, diff_lambda_q2_2, diff_lambda_k2_2, diff_subln_2, diff_w_o_2,
        ln_ffn_g_2, ln_ffn_b_2, ffn_w_up_2, ffn_w_down_2,
    )


_drawn_inputs = setup_inputs


def setup_inputs(seed=0):
    import zlib

    import numpy as np

    out = dict(_drawn_inputs(seed))
    spreads = {}
    factors = {'b_q_gain': 7.32,
     'kv_norm': 2.912,
     'k_gain': 7.903,
     'cmp_pos': 3.498,
     'mem_norm': 7.072,
     'mem_q_gain': 8.0,
     'mem_k_gain': 8.0,
     'mla_q_norm_2': 8.0,
     'mla_kv_norm_2': 8.0,
     'diff_lambda_q1_2': 3.583,
     'diff_lambda_q2_2': 8.0,
     'diff_lambda_k2_2': 8.0,
     'diff_subln_2': 21.617}
    for name, (base, spread) in spreads.items():
        noise = np.random.default_rng([zlib.crc32(name.encode()), seed]).standard_normal(out[name].shape)
        drawn = base * np.exp(spread * noise) if base else spread * noise
        out[name] = __import__('jax').numpy.asarray(drawn.astype(out[name].dtype))
    for name, factor in factors.items():
        out[name] = (out[name] * factor).astype(out[name].dtype)
    return out
```

```python
from contextlib import ExitStack
import math

import numpy as np
import concourse.bass as bass
from concourse import mybir

F32 = mybir.dt.float32
F32R = mybir.dt.float32r
I32 = mybir.dt.int32
ALU = mybir.AluOpType
ACT = mybir.ActivationFunctionType

P = 128
D = 1024
KT = D // P
S = 512
QT = S // P
MEM = 256
HD = 64
CONV = 768
CT = CONV // P
NH = 12
BR = 3
NC_ = 31
CSTR = 16
FF = 4096
FQ = FF // D
CW = 256
YR = 4
SLOT = KT * CW
NEG = -1e30
PI_IN = 3.1415925
ALPHA = (2 * 2) ** 0.25
LAM0 = 0.8 - 0.6 * math.exp(-0.3 * 1)
RMS_EPS, LN_EPS = 1e-6, 1e-5
MLA_Q, MLA_KV = 384, 256
MLA_SCALE = (128 + 64) ** -0.5
DIFF_SCALE = 64 ** -0.5

ROWS_A = [("mix0", 8), ("mix1", 8), ("kvn", 8), ("memn", 8), ("mlp0", 8), ("mlp1", 8),
          ("lmg0", 8), ("lmg1", 8), ("lmb0", 8), ("lmb1", 8), ("lfg0", 8), ("lfg1", 8),
          ("lfb0", 8), ("lfb1", 8)]
ROWS_B = [("conv", 18), ("qn", 3), ("kn", 2), ("sub", 1), ("bq", 1), ("kg", 3), ("mq", 2), ("mk", 2),
          ("pos", 32)]


def columns(rows):
    at, n = {}, 0
    for name, k in rows:
        at[name] = n
        n += k
    return at, n


COL_A, N_A = columns(ROWS_A)
COL_B, N_B = columns(ROWS_B)


class At:

    def __init__(self, fixed, i=None, per=0):
        if isinstance(i, int):
            fixed, i, per = fixed + i * per, None, 0
        self.fixed, self.i, self.per = fixed, i, per

    def __add__(self, k):
        return At(self.fixed + k, self.i, self.per)

    def __sub__(self, k):
        return self + -k

    @property
    def v(self):
        return self.fixed if self.i is None else self.i * self.per + self.fixed

    def slot(self, n):
        assert self.per % n == 0
        return self.fixed % n


class Tally:

    def __init__(self, sem):
        self.sem, self.n, self.i, self.per = sem, 0, None, 0

    def enter(self, i, per, first=1):
        self.i, self.per, self.began, self.first = i, per, self.n, first

    def leave(self, first, end):
        assert self.n - self.began == self.per, (self.n - self.began, self.per)
        self.n = self.began + self.per * (end - first)
        self.i = None

    def add(self, ins):
        ins.then_inc(self.sem, 1)
        self.n += 1
        return At(self.n - self.per * self.first if self.i is not None else self.n, self.i, self.per)


PHASES = [
    ("turn_x", dict(T=8, Q=8, R=1)), ("turn_mem", dict(T=8, Q=8, R=1)), ("turn_col", dict(T=2)),
    ("bias_v", dict(T=4)), ("norm_mem", dict(G=1, M=8)), ("mem", dict(C=4, T=6, Q=4, R=4, G=4)),
    ("bias_e", dict(T=12)), ("norm_a", dict(G=1, M=8)), ("a_in", dict(C=10, T=20, Q=2, R=2, G=2, M=6)),
    ("out0", dict(C=4, T=8, Q=8, R=1)), ("norm_f0", dict(G=1, M=8)),
    ("mlp0", dict(C=32, T=64, M=32, Q=8, R=1)), ("norm_kv", dict(G=1, M=8)),
    ("kv", dict(C=3, T=6, Q=2, R=2, G=2)), ("cmp", dict(M=4, C=4, T=2)), ("norm_b", dict(G=1, M=8)),
    ("b_in", dict(C=5, T=10, Q=8, R=8, G=8)), ("bias_c", dict(T=12)), ("cmp_out", dict(T=4, Q=1, R=1, G=1)),
    ("out1", dict(C=4, T=8, Q=8, R=1)), ("norm_f1", dict(G=1, M=8)), ("mlp1", dict(C=32, T=64, M=32)),
    ("split2", dict(M=8)), ("mla_a", dict(C=4, T=6, Q=5, R=2, G=2, M=5)),
    ("mla_b", dict(C=4, T=20)), ("rope_mla", dict(T=5)), ("mla_v", dict(C=1, T=8)), ("out2", dict(C=4, T=8)),
    ("ln2a", dict(Q=8, R=1, G=1, M=8, L=1)), ("mlp2", dict(C=32, T=64, M=32)),
    ("ln2b", dict(Q=8, R=1, G=1, M=8, L=1)), ("diff", dict(C=12, T=40)), ("out3", dict(C=4, T=8)),
    ("ln3a", dict(Q=8, R=1, G=1, M=8, L=1)), ("mlp3", dict(C=32, T=64, M=32)),
    ("ln3b", dict(Q=8, R=1, G=1, L=1)), ("turn_out", dict(T=8)), ("end", {}),
]
SUMS = {"turn_x": ("dve", [8]), "turn_mem": ("dve", [8]), "out0": ("dve", [8]), "mlp0": ("dve", [8]),
        "out1": ("dve", [8]), "mla_a": ("dve", [3, 2]), "mem": ("one", [1] * 4), "a_in": ("one", [1] * 2),
        "kv": ("one", [1] * 2), "cmp_out": ("one", [1]), "b_in": ("one", [1] * 8), "ln2a": ("dve", [8]),
        "ln2b": ("dve", [8]), "ln3a": ("dve", [8]), "ln3b": ("dve", [8])}
COUNT = dict(PHASES)


def bases():
    out, at = {}, dict(C=0, T=0, M=0, Q=0, R=0, G=0, L=0)
    for name, n in PHASES:
        out[name] = dict(at)
        for k, v in n.items():
            at[k] += v
    return out


BASE = bases()


def square_uses():
    uses, added = [], 0
    for name, _ in PHASES:
        who, sizes = SUMS.get(name, (None, []))
        for n, size in enumerate(sizes):
            for _ in range(size):
                if who == "dve":
                    added += 1
                    uses.append(("added", added))
                else:
                    uses.append(("stat_ready", BASE[name]["R"] + n + 1))
    return uses


SQUARE_USES = square_uses()
ROOT_SQUARES = [(SUMS[name][0], size) for name, _ in PHASES if name in SUMS for size in SUMS[name][1]]
N_CHUNKS = BASE["end"]["C"]
PIECES = {}
USED = {}
for _j in range(4):
    PIECES[BASE["out1"]["C"] + _j] = 3
for _j in range(3):
    PIECES[BASE["b_in"]["C"] + _j] = 4
    PIECES[BASE["mla_b"]["C"] + _j] = 3
for _j in (3, 4):
    PIECES[BASE["mla_b"]["C"] + _j] = 2
PIECES[BASE["mla_a"]["C"] + 3] = 2
PIECES[BASE["kv"]["C"] + 1] = 2
PIECES[BASE["kv"]["C"] + 2] = 2
USED[BASE["b_in"]["C"] + 3] = KT * 36
USED[BASE["mla_a"]["C"] + 1] = KT * 128
USED[BASE["mla_a"]["C"] + 3] = KT * 128
for _j in range(3):
    USED[BASE["mla_b"]["C"] + _j] = 3 * 512


def landed(c):
    done = sum(16 * PIECES.get(k, 1) for k in range(c.fixed % 2, c.fixed + 1, 2))
    return done if c.i is None else c.i * (8 * c.per) + done


def program(nc, a):
    ctx = ExitStack()
    with ctx:
        def sem(name):
            return ctx.enter_context(nc.semaphore(name))

        offset = [nc.sbuf_base + (-nc.sbuf_base) % 64]

        def sb(name, shape, dt, at=None):
            size = 4 * int(np.prod(shape[1:]))
            where = offset[0] if at is None else at
            if at is None:
                offset[0] += size + (-size) % 64
            t = nc.alloc_sbuf_tensor_at(name, shape, dt, offset=where)
            return t, where

        X, _ = sb("x", [P, KT, S], F32)
        HH, h_at = sb("operand_hi", [P, KT, S], F32R)
        HL, _ = sb("operand_lo", [P, KT, S], F32R)
        SC, _ = sb("scratch", [P, 16, S], F32, at=h_at)
        FH, f_at = sb("mixed_hi", [P, KT, S], F32R)
        FL, _ = sb("mixed_lo", [P, KT, S], F32R)
        raw, _ = sb("raw_weights", [P, 2, SLOT], F32)
        WH, _ = sb("weights_hi", [P, 2, SLOT], F32R)
        WL, _ = sb("weights_lo", [P, 2, SLOT], F32R)
        arena, _ = sb("arena", [P, 24, S], F32)
        mem_k, _ = sb("mem_k", [P, 2, 2, MEM], F32)
        mem_v, _ = sb("mem_v", [P, 2, 2, MEM], F32)
        ev, _ = sb("evacuated", [P, 2, S], F32)
        val, _ = sb("value", [P, 2, S], F32)
        SF, _ = sb("scratch_mixed", [P, 16, S], F32, at=f_at)
        w2s, _ = sb("compress_w2", [P, 2, 2, HD], F32)
        lam_in, _ = sb("lambda_in", [P, 4, HD], F32)
        sq, _ = sb("square", [P, 2, S], F32)
        rt, _ = sb("rstd", [P, 2, S], F32)
        spread, total = rt[:, 0, :], rt[:, 1, :]
        roots, _ = sb("roots", [P, 8 * BASE["end"]["R"]], F32)
        inverse, _ = sb("inverse_roots", [P, 8], F32)
        ident, _ = sb("ident", [P, P], F32)
        ones, _ = sb("ones", [P, P], F32)
        halves, _ = sb("half_ones", [P, P], F32)
        perm, _ = sb("perm", [P, P], F32)
        colA, _ = sb("columns_a", [P, N_A], F32)
        colB, _ = sb("columns_b", [P, N_B], F32)
        eps, _ = sb("eps", [P, 2], F32)
        gates, _ = sb("gates", [P, QT, 36], F32)
        small, _ = sb("small", [P, 160], F32)
        kc, _ = sb("kc", [P, 32], F32)
        vc, _ = sb("vc", [32, 2, HD], F32)
        cst, _ = sb("constant_columns", [P, 8], F32)
        lamt, _ = sb("lambda_columns", [P, 4], F32)
        assert offset[0] <= 229344 - 64, offset[0]

        pg = [ctx.enter_context(nc.psum_tensor(f"product{i}", [P, S], F32)) for i in range(2)]
        ST = [ctx.enter_context(nc.psum_tensor(f"stat{i}", [P, S], F32)) for i in range(2)]
        PS = [ctx.enter_context(nc.psum_tensor(f"scores{i}", [P, S], F32)) for i in range(2)]
        PT = [ctx.enter_context(nc.psum_tensor(f"turned{i}", [P, S], F32)) for i in range(2)]
        PO = ST

        vec_rows = nc.dram_tensor("bias_scratch", [NH, 2048], F32, kind="Internal").ap()

        QMEM0, QMEM1, QN, KS, KW, VSW, BIAS_E = 8, 6, 0, 8, 9, 10, 12

        const_loaded = sem("const_loaded")
        ident_loaded = sem("ident_loaded")
        rows_loaded = sem("rows_loaded")
        long_rows_loaded = sem("long_rows_loaded")
        eps_set = sem("eps_set")
        input_loaded = sem("input_loaded")
        mem_loaded = sem("mem_loaded")
        w_loaded = [sem(f"w_loaded{i}") for i in range(2)]
        w_hi = sem("w_hi")
        w_lo = sem("w_lo")
        acc_ready = sem("acc_ready")
        evacuated = sem("evacuated")
        ev_used = sem("ev_used")
        val_ready = sem("val_ready")
        val_hi = sem("val_hi")
        operand_ready = sem("operand_ready")
        sq_ready = sem("sq_ready")
        added = sem("added")
        stat_ready = sem("stat_ready")
        root_ready = sem("root_ready")
        spread_ready = sem("spread_ready")
        x_summed = sem("x_summed")
        x_scaled = sem("x_scaled")
        rstd_ready = sem("rstd_ready")
        norm_done = sem("norm_done")
        mean_ready = sem("mean_ready")
        centred = sem("centred")
        normed = sem("normed")
        trig_arg = sem("trig_arg")
        trig_ready = sem("trig_ready")
        pos_loaded = sem("pos_loaded")
        perm_loaded = sem("perm_loaded")
        mask_loaded = sem("mask_loaded")
        lam_in_ready = sem("lam_in_ready")
        lam_exp = sem("lam_exp")
        bias_stored = sem("bias_stored")
        hankel_loaded = sem("hankel_loaded")
        cmp_rows_loaded = sem("cmp_rows_loaded")
        gelu_in = sem("gelu_in")
        gelu_sigmoid = sem("gelu_sigmoid")
        hidden_ready = sem("hidden_ready")
        zeros_set = sem("zeros_set")
        x_final = sem("x_final")
        half_summed = sem("half_summed")
        rotated = sem("rotated")
        dve_step = Tally(sem("dve_step"))
        stored = sem("stored")

        gainA = lambda name, k: colA[:, COL_A[name] + k:COL_A[name] + k + 1]
        gainB = lambda name, k=0: colB[:, COL_B[name] + k:COL_B[name] + k + 1]

        kpn = lambda w: w.rearrange("(k p) n -> p k n", p=P)

        def load_chunk(sp, c, parts):
            s = c.slot(2)
            if c.fixed >= 2 or c.i is not None:
                sp.wait_ge(w_lo, (c - 1).v)
            for dst, src in parts:
                sp.dma_start(dst(raw[:, s, :]), src).then_inc(w_loaded[s], 16)

        def full(n, k=KT):
            return lambda r: r[:, 0:k * n].rearrange("p (k n) -> p k n", k=k)

        def split_hi(act, c):
            s, n = c.slot(2), USED.get(c.fixed, SLOT)
            act.wait_ge(w_loaded[s], landed(c))
            tiles = tiles_before(c)
            if tiles is not None:
                act.wait_ge(acc_ready, tiles.v)
            first = c.fixed - 2 - BASE["cmp"]["C"]
            if first in (0, 2):
                act.wait_ge(half_summed, first // 2 + 1)
            act.activation(WH[:, s, 0:n], raw[:, s, 0:n], ACT.Copy).then_inc(w_hi, 1)

        def split_lo(dve, c):
            s, n = c.slot(2), USED.get(c.fixed, SLOT)
            dve.wait_ge(w_hi, (c + 1).v)
            dve.tensor_tensor(WL[:, s, 0:n], raw[:, s, 0:n], WH[:, s, 0:n].bitcast(F32),
                              ALU.subtract).then_inc(w_lo, 1)

        chunk_tiles = []
        uneven = {"mem": [2, 1, 2, 1], "cmp": [0, 1, 0, 1], "b_in": [2, 2, 2, 1, 3],
                  "mla_a": [2, 1, 2, 1], "mla_b": [4, 4, 4, 8], "mla_v": [8], "diff": [2] * 8 + [6] * 4}
        for name, n in PHASES:
            per_chunk = uneven.get(name, [2] * n.get("C", 0))
            for k in range(n.get("C", 0)):
                chunk_tiles.append(BASE[name]["T"] + sum(per_chunk[:k + 1]))
        assert len(chunk_tiles) == N_CHUNKS

        def tiles_before(c):
            if c.i is None:
                return None if c.fixed < 2 else At(chunk_tiles[c.fixed - 2])
            return At(chunk_tiles[c.fixed - 2], c.i, 2 * c.per)

        def split_next(split, eng, c):
            if c.i is not None or c.fixed + 1 < N_CHUNKS:
                split(eng, c + 1)

        def token_blocks(N):
            return [(c0, min(P, N - c0)) for c0 in range(0, N, P)]

        def slot_view(s, k, n):
            return [w[:, s, 0:k * n].rearrange("p (k n) -> p k n", k=k) for w in (WH, WL)]

        def product3(pe, out, lhs, rhs, first, last):
            pe.matmul(out, lhs[0], rhs[0], start=first, stop=False)
            pe.matmul(out, lhs[0], rhs[1], start=False, stop=False)
            return pe.matmul(out, lhs[1], rhs[0], start=False, stop=last)

        def bank_for(pe, t):
            if t.fixed >= 2:
                pe.wait_ge(evacuated, (t - 1).v)
            return pg[t.slot(2)][:, :]

        def feature_tile(pe, t, w, j, A, kts, N=S, ready=None, first=True, last=True, off=0):
            out = bank_for(pe, t) if first else pg[t.slot(2)]
            for k in range(kts):
                if ready is not None:
                    pe.wait_ge(operand_ready, (ready + (k + 1)).v)
                ins = product3(pe, out[:, 0:N], [x[:, k, j * P:(j + 1) * P] for x in w],
                               [x[:, k + off, 0:N] for x in A], first and k == 0, last and k == kts - 1)
            return ins

        def token_tile(pe, t, w, cols, A, kts, toks):
            out = bank_for(pe, t)
            for n, q in enumerate(toks):
                for k in range(kts):
                    ins = product3(pe, out[:, n * cols:(n + 1) * cols],
                                   [x[:, k, q * P:(q + 1) * P] for x in A],
                                   [x[:, k, 0:cols] for x in w], k == 0, k == kts - 1)
            return ins

        def first_pair(pe, t, w, A, ready, N=S):
            out = [bank_for(pe, t), bank_for(pe, t + 1)]
            for k in range(KT):
                pe.wait_ge(operand_ready, (ready + (k + 1)).v)
                for j in range(2):
                    ins = product3(pe, out[j][:, 0:N], [x[:, k, j * P:(j + 1) * P] for x in w],
                                   [x[:, k, 0:N] for x in A], k == 0, k == KT - 1)
                    if k == KT - 1:
                        ins.then_inc(acc_ready, 1)

        def stats(pe, r, q, heads=1, N=S):
            who, size = ROOT_SQUARES[r]
            if who == "dve":
                pe.wait_ge(added, SQUARE_USES[q + size - 1][1])
                src = total
            else:
                pe.wait_ge(sq_ready, q + 1)
                src = sq[:, q % 2, :]
            if r >= 2:
                pe.wait_ge(root_ready, r - 1)
            for b, (c0, rows) in enumerate(token_blocks(N)):
                ins = pe.matmul(PT[r % 2][0:rows, b * heads:(b + 1) * heads], src[:, c0:c0 + rows],
                                halves[:, 0:P:HD] if heads == 2 else ones[:, 0:1], start=True, stop=True)
            ins.then_inc(stat_ready, 1)

        def turn_rstd(pe, g, N=S):
            pe.wait_ge(spread_ready, g + 1)
            if g >= 2:
                pe.wait_ge(norm_done, g - 1)
            for b, (c0, rows) in enumerate(token_blocks(N)):
                ins = pe.transpose(ST[g % 2][:, c0:c0 + rows], spread[0:rows, b * P:(b + 1) * P],
                                   ident[0:rows, 0:rows])
            ins.then_inc(rstd_ready, 1)

        def square(act, q, src, N=S):
            if q >= 2:
                who, n = SQUARE_USES[q - 2]
                act.wait_ge(dict(added=added, stat_ready=stat_ready)[who], n)
            act.activation(sq[:, q % 2, 0:N], src, ACT.Square).then_inc(sq_ready, 1)

        def root(act, r, width, which=0, heads=1, N=S):
            n = len(token_blocks(N)) * heads
            rows = token_blocks(N)[0][1]
            act.wait_ge(stat_ready, r + 1)
            act.activation(roots[0:rows, 8 * r:8 * r + n], PT[r % 2][0:rows, 0:n], ACT.Sqrt,
                           scale=1.0 / width, bias=eps[0:rows, which:which + 1]).then_inc(root_ready, 1)

        def evac(act, t, func=ACT.Copy, N=S, rows=P, scale=1.0):
            act.wait_ge(acc_ready, (t + 1).v)
            if t.fixed >= 2:
                act.wait_ge(ev_used, (t - 1).v)
            act.activation(ev[0:rows, t.slot(2), 0:N], pg[t.slot(2)][0:rows, 0:N], func,
                           scale=scale).then_inc(evacuated, 1)

        def high(act, m, dst, src):
            act.wait_ge(val_ready, (m + 1).v)
            act.activation(dst, src, ACT.Copy).then_inc(val_hi, 1)

        def dve_then(dve, ins):
            at = dve_step.add(ins)
            dve.wait_ge(dve_step.sem, at.v)

        def add_square(dve, q, r=None, N=S):
            n = SQUARE_USES[q][1]
            dve.wait_ge(sq_ready, q + 1)
            if n > 1:
                dve.wait_ge(added, n - 1)
            if r is None:
                dve.tensor_tensor(total[:, 0:N], total[:, 0:N], sq[:, q % 2, 0:N], ALU.add).then_inc(added, 1)
            else:
                if r:
                    dve.wait_ge(stat_ready, r)
                dve.tensor_copy(total[:, 0:N], sq[:, q % 2, 0:N]).then_inc(added, 1)

        def spread_rstd(dve, g, r, heads=1, N=S):
            blocks = token_blocks(N)
            n, rows = len(blocks) * heads, blocks[0][1]
            dve.wait_ge(root_ready, r + 1)
            dve_then(dve, dve.reciprocal(inverse[0:rows, 0:n], roots[0:rows, 8 * r:8 * r + n]))
            if g:
                dve.wait_ge(rstd_ready, g)
            dve.tensor_copy(spread[0:rows, 0:len(blocks) * P].rearrange("p (n c) -> p n c", n=n),
                            inverse[0:rows, 0:n].unsqueeze(2).broadcast_to([rows, n, P // heads]))\
                .then_inc(spread_ready, 1)

        def low(dve, m, dst, src, hi):
            dve.wait_ge(val_hi, (m + 1).v)
            dve.tensor_tensor(dst, src, hi.bitcast(F32), ALU.subtract).then_inc(operand_ready, 1)

        def vslot(m):
            return val[:, m.slot(2), :]

        def value_free(dve, m):
            if m.fixed >= 2:
                dve.wait_ge(operand_ready, (m - 1).v)

        def out_pe(pe, name):
            b = BASE[name]
            for c in range(4):
                pe.wait_ge(w_lo, b["C"] + c + 1)
                w = slot_view((b["C"] + c) % 2, KT, CW)
                for j in range(2):
                    t = At(b["T"] + 2 * c + j)
                    feature_tile(pe, t, w, j, (FH, FL), KT).then_inc(acc_ready, 1)

        def out_act(act, name):
            b = BASE[name]
            for c in range(4):
                split_next(split_hi, act, At(b["C"] + c))
                for k in (2 * c, 2 * c + 1):
                    if k:
                        x_tile_act(act, name, k - 1, b["T"] + k - 1)
                    evac(act, At(b["T"] + k))
            x_tile_act(act, name, KT - 1, b["T"] + KT - 1)
            x_end_act(act, name)

        def out_dve(dve, name):
            b = BASE[name]
            for c in range(4):
                split_next(split_lo, dve, At(b["C"] + c))
                for k in (2 * c, 2 * c + 1):
                    if k:
                        x_tile_dve(dve, name, k - 1, b["T"] + k - 1)
                    add_x(dve, At(b["T"] + k), k)
            x_tile_dve(dve, name, KT - 1, b["T"] + KT - 1)

        def add_x(dve, t, k):
            dve.wait_ge(evacuated, (t + 1).v)
            dve.tensor_tensor(X[:, k, :], X[:, k, :], ev[:, t.slot(2), :], ALU.add).then_inc(ev_used, 1)

        AFTER = {"turn_x": "square", "out0": "square", "mlp0": "square", "out1": "square", "mlp1": "split",
                 "out2": "sum", "mlp2": "sum", "out3": "sum", "mlp3": "sum"}

        def x_tile_act(act, name, k, t):
            if AFTER[name] == "square":
                act.wait_ge(ev_used, t + 1)
                square(act, BASE[name]["Q"] + k, X[:, k, :])
            elif AFTER[name] == "split":
                act.wait_ge(ev_used, t + 1)
                high(act, At(BASE["split2"]["M"] + k), HH[:, k, :], X[:, k, :])

        def x_end_act(act, name):
            if AFTER[name] == "square":
                root(act, BASE[name]["R"], D)

        def x_tile_dve(dve, name, k, t):
            if AFTER[name] == "square":
                add_square(dve, BASE[name]["Q"] + k, BASE[name]["R"] if k == 0 else None)
            elif AFTER[name] == "split":
                dve.engine_nop().then_inc(val_ready, 1)
                low(dve, At(BASE["split2"]["M"] + k), HL[:, k, :], X[:, k, :], HH[:, k, :])
            else:
                n = [name for name, kind in AFTER.items() if kind == "sum"].index(name) * KT + k
                dve.wait_ge(ev_used, t + 1)
                if n:
                    dve.wait_ge(x_summed, n)
                if k == 0:
                    dve.tensor_copy(total, X[:, 0, :]).then_inc(x_summed, 1)
                else:
                    dve.tensor_tensor(total, total, X[:, k, :], ALU.add).then_inc(x_summed, 1)

        def x_end_pe(pe, name):
            if AFTER[name] == "square":
                stats(pe, BASE[name]["R"], BASE[name]["Q"])

        def norm_act(act, name, dst, N=S, between={}):
            b = BASE[name]
            for k in range(KT):
                if k in between:
                    between[k](act)
                high(act, At(b["M"] + k), dst[:, k, 0:N], vslot(At(b["M"] + k))[:, 0:N])

        def norm_dve(dve, name, src, gain, r, N=S, between={}):
            b = BASE[name]
            spread_rstd(dve, b["G"], r, N=N)
            dve.wait_ge(rstd_ready, b["G"] + 1)
            for k in range(KT + 1):
                if k in between:
                    between[k](dve)
                if k < KT:
                    value_free(dve, At(b["M"] + k))
                    dve.scalar_tensor_tensor(vslot(At(b["M"] + k))[:, 0:N], src[:, k, 0:N],
                                             gainA(gain, k), ST[b["G"] % 2][:, 0:N],
                                             ALU.mult, ALU.mult).then_inc(val_ready, 1)
                if k:
                    m = At(b["M"] + k - 1)
                    low(dve, m, HL[:, k - 1, 0:N], vslot(m)[:, 0:N], HH[:, k - 1, 0:N])
            dve.engine_nop().then_inc(norm_done, 1)

        X_SCALED = {"mlp2": 2 * KT, "mlp3": 4 * KT}

        def mlp_pe(pe, name, i, last=False):
            b = BASE[name]
            m_in = b["M"] - 8
            for j in range(8):
                c = At(b["C"] + j, i, 8)
                pe.wait_ge(w_lo, (c + 1).v)
                w = slot_view(c.slot(2), KT, CW)
                if j == 0:
                    first_pair(pe, At(b["T"], i, 16), w, (HH, HL), At(m_in))
                    continue
                for n in range(2):
                    t = At(b["T"] + 2 * j + n, i, 16)
                    if j < 4:
                        feature_tile(pe, t, w, n, (HH, HL), KT).then_inc(acc_ready, 1)
                    else:
                        ready = At(b["M"], i, 8) if (j, n) == (4, 0) else None
                        feature_tile(pe, t, w, n, (FH, FL), KT, ready=ready).then_inc(acc_ready, 1)
            if last:
                x_end_pe(pe, name)

        def mlp_act(act, name, i, last=False):
            b = BASE[name]
            for j in range(8):
                c = At(b["C"] + j, i, 8)
                split_next(split_hi, act, c)
                for n in range(2):
                    t = At(b["T"] + 2 * j + n, i, 16)
                    if j < 4:
                        k = 2 * j + n
                        m = At(b["M"] + k, i, 8)
                        evac(act, t, ACT.Relu)
                        high(act, m, FH[:, k, :], vslot(m))
                    else:
                        k = 2 * (j - 4) + n
                        if last and k:
                            x_tile_act(act, name, k - 1, t.fixed - 1)
                        evac(act, t)
                if last and name == "mlp1" and j == 3:
                    trig_act(act, W_MLA, 0)
            if last:
                x_tile_act(act, name, KT - 1, t.fixed)
                x_end_act(act, name)

        def mlp_dve(dve, name, i, last=False):
            b = BASE[name]
            for j in range(8):
                c = At(b["C"] + j, i, 8)
                split_next(split_lo, dve, c)
                for n in range(2):
                    t = At(b["T"] + 2 * j + n, i, 16)
                    k = 2 * (j % 4) + n
                    if j < 4:
                        m = At(b["M"] + k, i, 8)
                        dve.wait_ge(evacuated, (t + 1).v)
                        value_free(dve, m)
                        dve.tensor_tensor(vslot(m), ev[:, t.slot(2), :], ev[:, t.slot(2), :],
                                          ALU.mult).then_inc(val_ready, 1)
                        low(dve, m, FL[:, k, :], vslot(m), FH[:, k, :])
                        dve.engine_nop().then_inc(ev_used, 1)
                    else:
                        dve.wait_ge(ev_used, At(b["T"], i, 16).v)
                        if name in X_SCALED:
                            dve.wait_ge(x_scaled, X_SCALED[name])
                        if last and k:
                            x_tile_dve(dve, name, k - 1, t.fixed - 1)
                        add_x(dve, t, k)
                if last and name == "mlp1" and j == 1:
                    trig_dve(dve, W_MLA, cst[:, 0:1], 0)
            if last:
                x_tile_dve(dve, name, KT - 1, t.fixed)


        def mlp_all(eng, name, part):
            with eng.Fori(0, FQ - 1) as i:
                part(eng, name, i)
            part(eng, name, FQ - 1, last=True)

        def turn_pe(pe, name, n, src, rows, N=P, after=None):
            for k in range(n):
                t = At(BASE[name]["T"] + k)
                out = bank_for(pe, t)
                blocks = src(k)
                for j, blk in enumerate(blocks):
                    ins = pe.transpose(out[:, j * N:j * N + rows], blk, ident[0:rows, 0:rows])
                ins.then_inc(acc_ready, 1)
                if after and k == 1:
                    after()

        def plain_act(act, name, n, N=S, rows=P):
            for k in range(n):
                evac(act, At(BASE[name]["T"] + k), N=N, rows=rows)

        def keep(dve, t, dst, src=None, N=S, rows=P):
            dve.wait_ge(evacuated, (t + 1).v)
            dve.tensor_copy(dst, ev[0:rows, t.slot(2), 0:N] if src is None else src).then_inc(ev_used, 1)

        def heads_pe(pe, name, heads, product, N=S):
            b = BASE[name]
            for n in range(len(heads) + 2):
                if n < len(heads):
                    product(n)
                if n >= 2 and heads[n - 2] is not None:
                    turn_rstd(pe, b["G"] + heads[n - 2], N)
                if 1 <= n <= len(heads) and heads[n - 1] is not None:
                    stats(pe, b["R"] + heads[n - 1], b["Q"] + heads[n - 1], 2, N)

        def heads_act(act, name, heads, evacuate, t0, N=S):
            b = BASE[name]
            for n in range(len(heads) + 1):
                if n < len(heads):
                    evacuate(n)
                    if heads[n] is not None:
                        t = At(t0 + n)
                        act.wait_ge(evacuated, (t + 1).v)
                        square(act, b["Q"] + heads[n], ev[:, t.slot(2), 0:N], N)
                if n and heads[n - 1] is not None:
                    root(act, b["R"] + heads[n - 1], HD, 0, 2, N)

        def heads_dve(dve, name, heads, before, finish, N=S):
            b = BASE[name]
            for n in range(len(heads) + 2):
                if n < len(heads):
                    before(n)
                if n >= 2:
                    finish(n - 2)
                if 1 <= n <= len(heads) and heads[n - 1] is not None:
                    spread_rstd(dve, b["G"] + heads[n - 1], b["R"] + heads[n - 1], 2, N)

        def head_norm_dve(dve, t, g, gain, dst, N=S):
            dve.wait_ge(evacuated, (t + 1).v)
            dve.wait_ge(rstd_ready, g + 1)
            dve.scalar_tensor_tensor(dst, ev[:, t.slot(2), 0:N], gain, ST[g % 2][:, 0:N],
                                     ALU.mult, ALU.mult).then_inc(ev_used, 1)
            dve.engine_nop().then_inc(norm_done, 1)

        MEM_HEADS = [0, 1, None, 2, 3, None]

        def mem_pe(pe):
            b = BASE["mem"]

            def product(n):
                l, j = n // 3, n % 3
                c = b["C"] + 2 * l + (j == 2)
                pe.wait_ge(w_lo, c + 1)
                w = slot_view(c % 2, KT, CW)
                if n == 0:
                    first_pair(pe, At(b["T"]), w, (HH, HL), At(BASE["norm_mem"]["M"]), MEM)
                elif j == 2:
                    token_tile(pe, At(b["T"] + n), w, CW, (HH, HL), KT, (0, 1)).then_inc(acc_ready, 1)
                elif n > 1:
                    feature_tile(pe, At(b["T"] + n), w, j, (HH, HL), KT, N=MEM).then_inc(acc_ready, 1)

            heads_pe(pe, "mem", MEM_HEADS, product, MEM)

        def mem_act(act):
            b = BASE["mem"]

            def evacuate(n):
                if n % 3 in (0, 2):
                    split_next(split_hi, act, At(b["C"] + 2 * (n // 3) + (n % 3 == 2)))
                evac(act, At(b["T"] + n), N=S if n % 3 == 2 else MEM)

            heads_act(act, "mem", MEM_HEADS, evacuate, b["T"], MEM)

        def mem_dve(dve):
            b = BASE["mem"]

            def before(n):
                if n % 3 in (0, 2):
                    split_next(split_lo, dve, At(b["C"] + 2 * (n // 3) + (n % 3 == 2)))

            def finish(n):
                l, j = n // 3, n % 3
                if j == 2:
                    keep(dve, At(b["T"] + n), mem_v[:, l, :, :].rearrange("p a b -> p (a b)"))
                else:
                    head_norm_dve(dve, At(b["T"] + n), b["G"] + MEM_HEADS[n], gainB("mk", l), mem_k[:, l, j, :],
                                  MEM)

            heads_dve(dve, "mem", MEM_HEADS, before, finish, MEM)

        def a_in_pe(pe):
            b = BASE["a_in"]

            def product(n):
                c, j = n // 2, n % 2
                pe.wait_ge(w_lo, b["C"] + c + 1)
                w = slot_view((b["C"] + c) % 2, KT, CW)
                if n == 0:
                    first_pair(pe, At(b["T"]), w, (HH, HL), At(BASE["norm_a"]["M"]))
                elif n > 1:
                    feature_tile(pe, At(b["T"] + n), w, j, (HH, HL), KT).then_inc(acc_ready, 1)

            for n in range(18):
                product(n)
            heads_pe(pe, "a_in", [0, 1], lambda n: product(18 + n))

        def a_in_act(act):
            b = BASE["a_in"]
            for c in range(9):
                split_next(split_hi, act, At(b["C"] + c))
                for j in range(2):
                    evac(act, At(b["T"] + 2 * c + j))
                    if c % 3 == 2:
                        k = 2 * (c // 3) + j
                        m = At(b["M"] + k)
                        high(act, m, FH[:, k, :], vslot(m))

            def evacuate(n):
                if n == 0:
                    split_next(split_hi, act, At(b["C"] + 9))
                evac(act, At(b["T"] + 18 + n))

            heads_act(act, "a_in", [0, 1], evacuate, b["T"] + 18)

        def a_in_dve(dve):
            b = BASE["a_in"]
            gate = lambda j: arena[:, j, :]
            cval = lambda j: arena[:, 2 + j, :]
            v = [arena[:, 4 + 2 * j:6 + 2 * j, :].rearrange("p a n -> p (a n)") for j in range(2)]
            conv = lambda k, ct: gainB("conv", k * CT + ct)
            for c in range(9):
                split_next(split_lo, dve, At(b["C"] + c))
                for j in range(2):
                    t = At(b["T"] + 2 * c + j)
                    ct = 2 * (c // 3) + j
                    if c % 3 == 0:
                        keep(dve, t, gate(j))
                    elif c % 3 == 1:
                        keep(dve, t, cval(j))
                    else:
                        if ct < 2:
                            dve_then(dve, dve.memset(v[j][:, 0:2], 0.0))
                        dve.wait_ge(evacuated, (t + 1).v)
                        dve.wait_ge(ev_used, t.v)
                        dve.tensor_tensor(v[j][:, 2:2 + S], cval(j), ev[:, t.slot(2), :],
                                          ALU.mult).then_inc(ev_used, 1)
                        dve.wait_ge(ev_used, (t + 1).v)
                        y = arena[:, 10 + j, :]
                        dve_then(dve, dve.tensor_scalar(y, v[j][:, 2:2 + S], conv(2, ct), None, ALU.mult))
                        dve_then(dve, dve.scalar_tensor_tensor(y, v[j][:, 1:1 + S], conv(1, ct), y,
                                                               ALU.mult, ALU.add))
                        dve_then(dve, dve.scalar_tensor_tensor(y, v[j][:, 0:S], conv(0, ct), y,
                                                               ALU.mult, ALU.add))
                        m = At(b["M"] + ct)
                        value_free(dve, m)
                        dve.tensor_tensor(vslot(m), y, gate(j), ALU.mult).then_inc(val_ready, 1)
                        low(dve, m, FL[:, ct, :], vslot(m), FH[:, ct, :])

            def before(n):
                if n == 0:
                    split_next(split_lo, dve, At(b["C"] + 9))

            def finish(n):
                head_norm_dve(dve, At(b["T"] + 18 + n), b["G"] + n, gainB("mq", 0), arena[:, QMEM0 + n, :])

            heads_dve(dve, "a_in", [0, 1], before, finish)

        def bias_v_pe(pe):
            for k in range(4):
                t = At(BASE["bias_v"]["T"] + k)
                pe.matmul(bank_for(pe, t)[0:NH, :], arena[0:33, 16, 0:NH], arena[0:33, 12 + k, :],
                          start=True, stop=True).then_inc(acc_ready, 1)

        def bias_e_pe(pe):
            pe.wait_ge(hankel_loaded, 16)
            for h in range(NH):
                t = At(BASE["bias_e"]["T"] + h)
                pe.matmul(bank_for(pe, t), perm[:, :], arena[:, BIAS_E + h, :], start=True,
                          stop=True).then_inc(acc_ready, 1)

        def bias_c_pe(pe):
            pe.wait_ge(cmp_rows_loaded, 16 * 4)
            pe.wait_ge(perm_loaded, 16 * 2)
            for n in range(12):
                t = At(BASE["bias_c"]["T"] + n)
                hg, i = n // 4, n % 4
                pe.matmul(bank_for(pe, t)[:, 0:124], SF[0:124, 8 + hg, i * P:(i + 1) * P],
                          perm[0:124, 0:124], start=True, stop=True).then_inc(acc_ready, 1)

        KV_HEADS = [None, None, 0, 1, None, None]

        def kv_pe(pe):
            b = BASE["kv"]

            def product(n):
                c, j = n // 2, n % 2
                pe.wait_ge(w_lo, b["C"] + c + 1)
                w = slot_view((b["C"] + c) % 2, KT, CW)
                t = At(b["T"] + n)
                if n == 0:
                    first_pair(pe, t, w, (HH, HL), At(BASE["norm_kv"]["M"]))
                elif c == 1:
                    feature_tile(pe, t, w, j, (HH, HL), KT).then_inc(acc_ready, 1)
                elif c == 2:
                    token_tile(pe, t, w, CW, (HH, HL), KT, (2 * j, 2 * j + 1)).then_inc(acc_ready, 1)

            heads_pe(pe, "kv", KV_HEADS, product)

        def kv_act(act):
            b = BASE["kv"]

            def evacuate(n):
                if n % 2 == 0:
                    split_next(split_hi, act, At(b["C"] + n // 2))
                if n >= 4:
                    for m in (2 * n - 8, 2 * n - 7):
                        cmp_operand_act(act, m)
                evac(act, At(b["T"] + n))

            heads_act(act, "kv", KV_HEADS, evacuate, b["T"])

        def kv_dve(dve):
            b = BASE["kv"]

            def before(n):
                if n % 2 == 0:
                    split_next(split_lo, dve, At(b["C"] + n // 2))
                if n >= 4:
                    for m in (2 * n - 8, 2 * n - 7):
                        cmp_operand_dve(dve, m)

            def finish(n):
                t, j = At(b["T"] + n), n % 2
                if n < 2:
                    dve.wait_ge(evacuated, (t + 1).v)
                    U = SF[:, 4 + 2 * j:6 + 2 * j, :]
                    for g in range(2):
                        src = ev[g * HD:(g + 1) * HD, t.slot(2), :]
                        dve_step.add(dve.tensor_copy(U[0:HD, g, :], src))
                        ins = dve.tensor_copy(U[HD:P, g, 0:S - 1], src[:, 1:S])
                        if g == 0:
                            dve_step.add(ins)
                    ins.then_inc(ev_used, 1)
                    dve.wait_ge(dve_step.sem, dve_step.n)
                elif n < 4:
                    head_norm_dve(dve, t, b["G"] + j, gainB("kg", 1 + j), arena[:, KS + j, :])
                else:
                    keep(dve, t, arena[:, VSW + j, :])

            heads_dve(dve, "kv", KV_HEADS, before, finish)

        def flat_view(x):
            return x.rearrange("p (t n) -> p t n", n=HD)

        part = lambda kv, k: SF[0:62, 12 + 2 * kv + k // 2, (k % 2) * CW:(k % 2 + 1) * CW]
        hid = lambda kv, j, g: SF[:, 4 + 2 * kv, j * HD + g * NC_:j * HD + (g + 1) * NC_]

        def cmp_pe(pe):
            b = BASE["cmp"]
            for c in range(4):
                kv, h = c // 2, c % 2
                pe.wait_ge(w_lo, b["C"] + c + 1)
                pe.wait_ge(operand_ready, b["M"] + c + 1)
                w = slot_view((b["C"] + c) % 2, KT, CW)
                t = At(b["T"] + kv)
                out = bank_for(pe, t) if h == 0 else pg[t.slot(2)]
                for k in range(KT):
                    ins = product3(pe, out[0:62, 0:CW], [x[:, c, k * HD:k * HD + 62] for x in (FH, FL)],
                                   [x[:, k, :] for x in w], h == 0 and k == 0, h == 1 and k == KT - 1)
                ins.then_inc(acc_ready if h == 1 else half_summed, 1)

        def cmp_out_pe(pe):
            b = BASE["cmp_out"]
            for kv in range(2):
                pe.wait_ge(hidden_ready, kv + 1)
                out = bank_for(pe, At(b["T"] + kv))
                for j in range(2):
                    ins = pe.transpose(out[:, j * HD:j * HD + 62], part(kv, 3)[:, j * P:(j + 1) * P],
                                       ident[0:62, 0:62])
                ins.then_inc(acc_ready, 1)

            def product(n):
                t = At(b["T"] + 2 + n)
                pe.wait_ge(ev_used, b["T"] + n + 1)
                out = bank_for(pe, t)
                for g in range(2):
                    for j in range(2):
                        if n == 0:
                            ins = pe.matmul(out[g * HD:(g + 1) * HD, 0:NC_], w2s[:, 0, j, :], hid(0, j, g),
                                            start=j == 0, stop=j == 1)
                        else:
                            ins = pe.matmul(out[0:NC_, g * HD:(g + 1) * HD], hid(1, j, g), w2s[:, 1, j, :],
                                            start=j == 0, stop=j == 1)
                ins.then_inc(acc_ready, 1)

            heads_pe(pe, "cmp_out", [0, None], product, NC_)

        def cmp_operand_act(act, m):
            high(act, At(BASE["cmp"]["M"] + m), FH[:, m, :], vslot(At(BASE["cmp"]["M"] + m)))

        def cmp_act(act):
            b = BASE["cmp"]
            for kv in range(2):
                evac(act, At(b["T"] + kv), N=CW, rows=62)
            for kv in range(2):
                act.wait_ge(gelu_in, kv + 1)
                act.activation(part(kv, 2), part(kv, 1), ACT.Sigmoid,
                               scale=2 * math.sqrt(2 / math.pi)).then_inc(gelu_sigmoid, 1)

        def cmp_out_act(act):
            b = BASE["cmp_out"]
            for kv in range(2):
                evac(act, At(b["T"] + kv), N=P)
            heads_act(act, "cmp_out", [0, None],
                      lambda n: evac(act, At(b["T"] + 2 + n), N=(NC_, P)[n], rows=(P, NC_)[n]), b["T"] + 2, NC_)

        def cmp_operand_dve(dve, m):
            kv, h = m // 2, m % 2
            mm = At(BASE["cmp"]["M"] + m)
            flat = flat_view(vslot(mm))
            pos = colB[:, COL_B["pos"] + 16 * kv + 8 * h:COL_B["pos"] + 16 * kv + 8 * h + 8]
            value_free(dve, mm)
            dve_step.add(dve.memset(flat[:, :, 62:64], 0.0))
            for g in range(2):
                win = SF[:, 4 + 2 * kv + g, 16 * h:16 * h + 16 * NC_]\
                    .rearrange("p (c t two) -> p t c two", t=8, two=2)[:, :, :, 0]
                ins = dve.tensor_tensor(flat[:, :, g * NC_:(g + 1) * NC_], win,
                                        pos.unsqueeze(2).broadcast_to([P, 8, NC_]), ALU.add)
                if g == 0:
                    dve_step.add(ins)
            dve.wait_ge(dve_step.sem, dve_step.n)
            ins.then_inc(val_ready, 1)
            low(dve, mm, FL[:, m, :], vslot(mm), FH[:, m, :])

        def cmp_dve(dve):
            b = BASE["cmp"]
            for kv in range(2):
                t = At(b["T"] + kv)
                keep(dve, t, part(kv, 0), N=CW, rows=62)
                dve.wait_ge(ev_used, (t + 1).v)
                dve_then(dve, dve.tensor_tensor(part(kv, 1), part(kv, 0), part(kv, 0), ALU.mult))
                dve_then(dve, dve.tensor_scalar(part(kv, 1), part(kv, 1), 0.044715, 1.0, ALU.mult, ALU.add))
                dve.tensor_tensor(part(kv, 1), part(kv, 1), part(kv, 0), ALU.mult).then_inc(gelu_in, 1)
            for kv in range(2):
                dve.wait_ge(gelu_sigmoid, kv + 1)
                dve.tensor_tensor(part(kv, 3), part(kv, 2), part(kv, 0), ALU.mult).then_inc(hidden_ready, 1)

        def cmp_out_dve(dve):
            b = BASE["cmp_out"]
            for kv in range(2):
                keep(dve, At(b["T"] + kv), SF[:, 4 + 2 * kv, 0:P], N=P)

            def finish(n):
                t = At(b["T"] + 2 + n)
                if n == 0:
                    head_norm_dve(dve, t, b["G"], gainB("kg", 0), kc[:, 0:NC_], NC_)
                else:
                    keep(dve, t, vc[0:NC_, :, :].rearrange("p g d -> p (g d)"), N=P, rows=NC_)

            heads_dve(dve, "cmp_out", [0, None], lambda n: None, finish, NC_)

        B_CHUNK = [0, 0, 1, 1, 2, 2, 3, 4, 4, 4]
        B_HEADS = [0, 1, 2, 3, 4, 5, None, 6, 7, None]

        def b_in_pe(pe):
            b = BASE["b_in"]

            def product(n):
                c = b["C"] + B_CHUNK[n]
                pe.wait_ge(w_lo, c + 1)
                t = At(b["T"] + n)
                if n == 0:
                    first_pair(pe, t, slot_view(c % 2, KT, CW), (HH, HL), At(BASE["norm_b"]["M"]))
                elif n == 6:
                    out = bank_for(pe, t)
                    w = slot_view(c % 2, KT, 36)
                    for k in range(KT):
                        ins = product3(pe, out[0:36, :], [x[:, k, :] for x in w],
                                       [x[:, k, :] for x in (HH, HL)], k == 0, k == KT - 1)
                    ins.then_inc(acc_ready, 1)
                elif n == 9:
                    pe.wait_ge(ev_used, b["T"] + 7)
                    out = bank_for(pe, t)
                    for q in range(QT):
                        ins = pe.transpose(out[:, q * 36:(q + 1) * 36], val[0:36, 0, q * P:(q + 1) * P],
                                           ident[0:36, 0:36])
                    ins.then_inc(acc_ready, 1)
                elif n > 1:
                    feature_tile(pe, t, slot_view(c % 2, KT, CW), (n + (n > 6)) % 2, (HH, HL), KT)\
                        .then_inc(acc_ready, 1)

            heads_pe(pe, "b_in", B_HEADS, product)

        def b_in_act(act):
            b = BASE["b_in"]

            def evacuate(n):
                if n == 0 or B_CHUNK[n] != B_CHUNK[n - 1]:
                    split_next(split_hi, act, At(b["C"] + B_CHUNK[n]))
                t = At(b["T"] + n)
                if n == 6:
                    evac(act, t, ACT.Sigmoid, rows=36)
                elif n == 9:
                    evac(act, t, N=QT * 36)
                else:
                    evac(act, t)

            heads_act(act, "b_in", B_HEADS, evacuate, b["T"])

        def b_in_dve(dve):
            b = BASE["b_in"]

            def before(n):
                if n == 0 or B_CHUNK[n] != B_CHUNK[n - 1]:
                    split_next(split_lo, dve, At(b["C"] + B_CHUNK[n]))

            def finish(n):
                t = At(b["T"] + n)
                if n == 6:
                    keep(dve, t, val[0:36, 0, :], rows=36)
                elif n == 9:
                    keep(dve, t, gates[:, :, :].rearrange("p a b -> p (a b)"), N=QT * 36)
                else:
                    slot, gain = (QN + n, gainB("bq")) if n < 6 else (QMEM1 + n - 7, gainB("mq", 1))
                    head_norm_dve(dve, t, b["G"] + B_HEADS[n], gain, arena[:, slot, :])

            heads_dve(dve, "b_in", B_HEADS, before, finish)

        def plain_dve(dve, name, n, dst, N=S, rows=P):
            for k in range(n):
                keep(dve, At(BASE[name]["T"] + k), dst(k), N=N, rows=rows)

        def ln_pe(pe, name):
            b = BASE[name]
            pe.wait_ge(x_summed, (b["L"] + 1) * KT)
            pe.matmul(PS[0][:, :], ones[:, :], total, start=True, stop=True).then_inc(mean_ready, 1)
            stats(pe, b["R"], b["Q"])
            turn_rstd(pe, b["G"])

        def ln_act(act, name, beta):
            b = BASE[name]
            for k in range(KT):
                act.wait_ge(centred, b["L"] * KT + k + 1)
                square(act, b["Q"] + k, X[:, k, :])
            root(act, b["R"], D, 1)
            for k in range(KT):
                if "M" in COUNT[name]:
                    m = At(b["M"] + k)
                    act.wait_ge(val_ready, (m + 1).v)
                    act.activation(HH[:, k, :], X[:, k, :], ACT.Identity,
                                   bias=gainA(beta, k)).then_inc(val_hi, 1)
                else:
                    act.wait_ge(normed, k + 1)
                    act.activation(X[:, k, :], X[:, k, :], ACT.Identity, bias=gainA(beta, k)).then_inc(x_final, 1)

        def ln_dve(dve, name, g, beta):
            b = BASE[name]
            more = "M" in COUNT[name]
            dve.wait_ge(mean_ready, b["L"] + 1)
            for k in range(KT):
                dve.scalar_tensor_tensor(X[:, k, :], PS[0][:, :], -1.0 / D, X[:, k, :], ALU.mult,
                                         ALU.add).then_inc(centred, 1)
                if k > 1:
                    add_square(dve, b["Q"] + k - 2, b["R"] if k == 2 else None)
            for k in (KT - 2, KT - 1):
                add_square(dve, b["Q"] + k)
            spread_rstd(dve, b["G"], b["R"])
            dve.wait_ge(rstd_ready, b["G"] + 1)
            dve.wait_ge(centred, (b["L"] + 1) * KT)
            for k in range(KT + 1):
                if k < KT:
                    dve.scalar_tensor_tensor(X[:, k, :], X[:, k, :], gainA(g, k), ST[b["G"] % 2][:, :],
                                             ALU.mult, ALU.mult).then_inc(val_ready if more else normed, 1)
                if k and more:
                    m = At(b["M"] + k - 1)
                    dve.wait_ge(val_hi, (m + 1).v)
                    dve.scalar_tensor_tensor(HL[:, k - 1, :], X[:, k - 1, :], gainA(beta, k - 1),
                                             HH[:, k - 1, :].bitcast(F32), ALU.add,
                                             ALU.subtract).then_inc(operand_ready, 1)
            dve.engine_nop().then_inc(norm_done, 1)

        def scale_pool(pool, name, beta=None):
            for k in range(KT):
                pool.wait_ge(operand_ready, BASE[name]["M"] + k + 1)
                if beta is None:
                    ins = pool.tensor_scalar(X[:, k, :], X[:, k, :], ALPHA, None, ALU.mult)
                else:
                    ins = pool.tensor_scalar(X[:, k, :], X[:, k, :], gainA(beta, k), ALPHA, ALU.add, ALU.mult)
                ins.then_inc(x_scaled, 1)

        def trig_dve(dve, W, freq, n):
            two_pi = 2 * math.pi
            parts, left = [], two_pi
            for bits in (5, 13, 21):
                part = math.floor(left * 2 ** bits) / 2 ** bits
                parts.append(part)
                left -= part
            parts.append(float(np.float32(left)))
            dve.wait_ge(pos_loaded, 16 * (n + 1))
            dve_then(dve, dve.tensor_copy(W[:, 3, :], W[:, 2, :].bitcast(I32)))
            dve_then(dve, dve.tensor_scalar(W[:, 3, :], W[:, 3, :], freq, None, ALU.mult))
            for j, quarter in enumerate((0.25, 0.0)):
                dve_then(dve, dve.tensor_scalar(W[:, 4, :], W[:, 3, :], 1 / two_pi, quarter,
                                                ALU.mult, ALU.add))
                dve_then(dve, dve.tensor_scalar(W[:, 4, :], W[:, 4, :], 12582912.0, -12582912.0,
                                                ALU.add, ALU.add))
                src = W[:, 3, :]
                for part in parts:
                    dve_then(dve, dve.scalar_tensor_tensor(W[:, j, :], W[:, 4, :], -part, src,
                                                           ALU.mult, ALU.add))
                    src = W[:, j, :]
                if quarter:
                    dve_then(dve, dve.tensor_scalar(W[:, j, :], W[:, j, :], math.pi / 2, None, ALU.add))
                dve.tensor_scalar(W[:, j, :], W[:, j, :], PI_IN, -PI_IN, ALU.min,
                                  ALU.max).then_inc(trig_arg, 1)

        def trig_act(act, W, n):
            for j in range(2):
                act.wait_ge(trig_arg, 2 * n + j + 1)
                act.activation(W[:, j, :], W[:, j, :], ACT.Sin).then_inc(trig_ready, 1)

        def rope_pe(pe, t, src):
            pe.matmul(bank_for(pe, t), perm[:, :], src, start=True, stop=True).then_inc(acc_ready, 1)

        def rope_dve(dve, t, W, src, dst):
            dve.wait_ge(evacuated, (t + 1).v)
            dve_step.add(dve.tensor_tensor(val[:, 0, :], src, W[:, 0, :], ALU.mult))
            dve.tensor_tensor(sq[:, 1, :], ev[:, t.slot(2), :], W[:, 1, :], ALU.mult).then_inc(ev_used, 1)
            dve.wait_ge(dve_step.sem, dve_step.n)
            dve.wait_ge(ev_used, (t + 1).v)
            dve_then(dve, dve.tensor_tensor(dst, val[:, 0, :], sq[:, 1, :], ALU.add))

        MLA_CHUNK = [0, 0, 1, 2, 2, 3]

        def mla_a_pe(pe):
            b = BASE["mla_a"]
            for n, c in enumerate(MLA_CHUNK):
                pe.wait_ge(w_lo, b["C"] + c + 1)
                w = slot_view((b["C"] + c) % 2, KT, CW if c in (0, 2) else P)
                if n == 0:
                    first_pair(pe, At(b["T"]), w, (HH, HL), At(BASE["split2"]["M"]))
                elif n > 1:
                    feature_tile(pe, At(b["T"] + n), w, [0, 1, 0, 0, 1, 0][n], (HH, HL), KT).then_inc(acc_ready, 1)
                if n == 3:
                    stats(pe, b["R"], b["Q"])
                if n == 4:
                    turn_rstd(pe, b["G"])
            stats(pe, b["R"] + 1, b["Q"] + 3)
            turn_rstd(pe, b["G"] + 1)

        def mla_a_act(act):
            b = BASE["mla_a"]
            for n, c in enumerate(MLA_CHUNK):
                if n == 0 or c != MLA_CHUNK[n - 1]:
                    split_next(split_hi, act, At(b["C"] + c))
                t = At(b["T"] + n)
                evac(act, t)
                if n < 5:
                    act.wait_ge(evacuated, (t + 1).v)
                    square(act, b["Q"] + n, ev[:, t.slot(2), :])
                if n == 3:
                    root(act, b["R"], MLA_Q)
            root(act, b["R"] + 1, MLA_KV)
            for k in range(5):
                m = At(b["M"] + k)
                high(act, m, FH[:, k, :], vslot(m))

        def mla_a_dve(dve):
            b = BASE["mla_a"]
            for n, c in enumerate(MLA_CHUNK):
                if n == 0 or c != MLA_CHUNK[n - 1]:
                    split_next(split_lo, dve, At(b["C"] + c))
                keep(dve, At(b["T"] + n), arena[:, n, :] if n < 5 else SF[:, 5, :])
                if n < 5:
                    add_square(dve, b["Q"] + n, {0: b["R"], 3: b["R"] + 1}.get(n))
                if n == 3:
                    spread_rstd(dve, b["G"], b["R"])
            spread_rstd(dve, b["G"] + 1, b["R"] + 1)
            dve.wait_ge(ev_used, b["T"] + 6)
            for k in range(6):
                if k < 5:
                    m = At(b["M"] + k)
                    g = b["G"] + (k >= 3)
                    dve.wait_ge(rstd_ready, g + 1)
                    gain = gainB("qn", k) if k < 3 else gainB("kn", k - 3)
                    value_free(dve, m)
                    dve.scalar_tensor_tensor(vslot(m), arena[:, k, :], gain, ST[g % 2][:, :], ALU.mult,
                                             ALU.mult).then_inc(val_ready, 1)
                if k:
                    m = At(b["M"] + k - 1)
                    low(dve, m, FL[:, k - 1, :], vslot(m), FH[:, k - 1, :])
                if k in (2, 4):
                    dve.engine_nop().then_inc(norm_done, 1)

        V_MLA = arena[:, 16:24, :].rearrange("p (t a) n -> p t (a n)", t=QT)

        def mla_b_pe(pe):
            b = BASE["mla_b"]
            t = At(b["T"])
            for c in range(4):
                pe.wait_ge(w_lo, b["C"] + c + 1)
                s = (b["C"] + c) % 2
                if c == 0:
                    pe.wait_ge(operand_ready, BASE["mla_a"]["M"] + 5)
                for j in range(MLA_B_TILES[c]):
                    if c < 3:
                        feature_tile(pe, t, slot_view(s, 3, 512), j, (FH, FL), 3).then_inc(acc_ready, 1)
                    else:
                        feature_tile(pe, t, slot_view(s, 2, 1024), j, (FH, FL), 2, off=3)\
                            .then_inc(acc_ready, 1)
                    t = t + 1

        MLA_B_TILES = [4, 4, 4, 8]

        def mla_b_act(act):
            b, n = BASE["mla_b"], 0
            for c in range(4):
                split_next(split_hi, act, At(b["C"] + c))
                for j in range(MLA_B_TILES[c]):
                    evac(act, At(b["T"] + n))
                    n += 1

        def mla_b_dve(dve):
            b, n = BASE["mla_b"], 0
            for c in range(4):
                split_next(split_lo, dve, At(b["C"] + c))
                for j in range(MLA_B_TILES[c]):
                    dst = arena[:, 4 * c + j, :] if c < 2 else SC[:, 11 + j, :] if c == 2 else \
                        arena[:, 8 + j, :]
                    keep(dve, At(b["T"] + n), dst)
                    n += 1

        ROPE_MLA = [(SC[:, 11 + k, :] if k < 4 else SF[:, 5, :], SC[:, 11 + k, :]) for k in range(5)]
        W_MLA = arena[:, 19:24, :]

        def mla_v_pe(pe):
            pe.wait_ge(perm_loaded, 48)
            pe.wait_ge(ev_used, BASE["mla_b"]["T"] + 12)
            for k in range(5):
                rope_pe(pe, At(BASE["rope_mla"]["T"] + k), ROPE_MLA[k][0])
            b = BASE["mla_v"]
            pe.wait_ge(w_lo, b["C"] + 1)
            w = slot_view(b["C"] % 2, 2, 1024)
            for n in range(8):
                t, q, part = At(b["T"] + n), n // 2, n % 2
                out = bank_for(pe, t)
                for k in range(2):
                    ins = product3(pe, out[:, :], [x[:, 3 + k, q * P:(q + 1) * P] for x in (FH, FL)],
                                   [x[:, k, part * S:(part + 1) * S] for x in w], k == 0, k == 1)
                ins.then_inc(acc_ready, 1)

        def mla_v_act(act):
            plain_act(act, "rope_mla", 5)
            split_next(split_hi, act, At(BASE["mla_v"]["C"]))
            plain_act(act, "mla_v", 8)

        def mla_v_dve(dve):
            dve.wait_ge(trig_ready, 2)
            for k, (src, dst) in enumerate(ROPE_MLA):
                rope_dve(dve, At(BASE["rope_mla"]["T"] + k), W_MLA, src, dst)
            dve.engine_nop().then_inc(rotated, 1)
            split_next(split_lo, dve, At(BASE["mla_v"]["C"]))
            plain_dve(dve, "mla_v", 8, lambda n: V_MLA[:, n // 2, (n % 2) * S:(n % 2 + 1) * S])

        V_DIFF = V_MLA
        D_EXTRA = ["v", 0, 1, "v", 2, 3]

        def diff_pe(pe):
            b = BASE["diff"]
            for c in range(8):
                pe.wait_ge(w_lo, b["C"] + c + 1)
                w = slot_view((b["C"] + c) % 2, KT, CW)
                if c == 0:
                    first_pair(pe, At(b["T"]), w, (HH, HL), At(BASE["ln2b"]["M"]))
                    continue
                for j in range(2):
                    feature_tile(pe, At(b["T"] + 2 * c + j), w, j, (HH, HL), KT).then_inc(acc_ready, 1)
            pe.wait_ge(perm_loaded, 16 * 4)
            for c in range(4):
                pe.wait_ge(w_lo, b["C"] + 8 + c + 1)
                w = slot_view((b["C"] + 8 + c) % 2, KT, CW)
                half = 0
                for j, kind in enumerate(D_EXTRA):
                    t = At(b["T"] + 16 + 6 * c + j)
                    if kind == "v":
                        token_tile(pe, t, w, CW, (HH, HL), KT, (2 * half, 2 * half + 1))\
                            .then_inc(acc_ready, 1)
                        half += 1
                    else:
                        n = 4 * c + kind
                        pe.wait_ge(ev_used, b["T"] + n + 1)
                        rope_pe(pe, t, arena[:, n, :])

        def diff_act(act):
            b = BASE["diff"]
            for c in range(12):
                split_next(split_hi, act, At(b["C"] + c))
                if c < 8:
                    for j in range(2):
                        evac(act, At(b["T"] + 2 * c + j))
                    if c == 3:
                        trig_act(act, SF, 1)
                else:
                    for j in range(6):
                        evac(act, At(b["T"] + 16 + 6 * (c - 8) + j))

        def diff_dve(dve):
            b = BASE["diff"]
            for c in range(12):
                split_next(split_lo, dve, At(b["C"] + c))
                if c < 8:
                    for j in range(2):
                        keep(dve, At(b["T"] + 2 * c + j), arena[:, 2 * c + j, :])
                    if c == 3:
                        trig_dve(dve, SF, cst[:, 1:2], 1)
                    if c == 7:
                        dve.wait_ge(trig_ready, 4)
                        dve.wait_ge(ev_used, b["T"] + 16)
                else:
                    half = 0
                    for j, kind in enumerate(D_EXTRA):
                        t = At(b["T"] + 16 + 6 * (c - 8) + j)
                        if kind == "v":
                            dve.wait_ge(evacuated, (t + 1).v)
                            dve.tensor_copy(V_DIFF[:, 2 * half:2 * half + 2, (c - 8) * CW:(c - 7) * CW],
                                            ev[:, t.slot(2), :].rearrange("p (a n) -> p a n", a=2))\
                                .then_inc(ev_used, 1)
                            half += 1
                        else:
                            n = 4 * (c - 8) + kind
                            rope_dve(dve, t, SF, arena[:, n, :], arena[:, n, :])

        head_rows = lambda h: cst[:, 4 + h:5 + h]

        def attention(at):
            n, units, times = len(at["units"]), at["units"], at["times"]
            nm = at["name"]
            groups = sorted(at["groups"], key=lambda g: g["last"] + (2 if g["reader"] == 2 else 0))
            copies_of = [len(group["copies"](0)) for group in groups]
            first_order = sorted(range(len(groups)), key=lambda g: groups[g]["need"])
            staged = sem(nm + "_staged")
            scores_ready = sem(nm + "_scores_ready")
            logits_ready = sem(nm + "_logits_ready")
            probs_ready = sem(nm + "_probs_ready")
            turned_ready = sem(nm + "_turned_ready")
            turned_copied = sem(nm + "_turned_copied")
            weights_ready = sem(nm + "_weights_ready")
            out_ready = sem(nm + "_out_ready")
            out_used = sem(nm + "_out_used")
            y_summed = sem(nm + "_y_summed")
            y_rstd = sem(nm + "_y_rstd")
            y_ready = sem(nm + "_y_ready")
            y_turned = sem(nm + "_y_turned")
            y_hi = sem(nm + "_y_hi")
            y_lo = sem(nm + "_y_lo")
            ys = [u for u in range(n) if units[u].get("last")]
            ny = len(ys)
            normed_out = at.get("norm", False)
            LP = lambda u: SC[:, at["LP"] + u % 4, :]
            PTs = lambda u: val[:, u % 2, :]
            y = lambda k: rt[:, 0, (k % YR) * P:(k % YR + 1) * P]
            junk = lambda k: rt[:, 1, (k % YR) * P:(k % YR + 1) * P]
            col = lambda kind, u: small[:, kind * n + u:kind * n + u + 1]
            ycol = lambda kind, k: small[:, 4 * n + kind * ny + k:4 * n + kind * ny + k + 1]
            nk = lambda u: units[u]["nk"]
            kts = lambda u: [(b * P, min(P, nk(u) - b * P)) for b in range((nk(u) + P - 1) // P)]
            lag = 3 if normed_out else 0
            gain = at.get("gain", 1.0)
            assert n % 4 == 0 and ny % YR == 0 and 4 * n + 2 * ny <= 150

            def count(u, i, per=n):
                return At(u + 1, i, per)

            def wait_free(eng, sem_, u, ring, i, per=n):
                at_ = At(u + 1 - ring, i, per)
                if at_.i is not None or at_.fixed > 0:
                    eng.wait_ge(sem_, at_.v)

            def wait_staged(eng, reader, u, i):
                wanted = [g for g, group in enumerate(groups) if (group["reader"], group["need"]) == (reader, u)]
                if wanted and isinstance(i, int) and i == 0:
                    last = max(first_order.index(g) for g in wanted)
                    eng.wait_ge(staged, sum(copies_of[g] for g in first_order[:last + 1]))
                elif wanted:
                    eng.wait_ge(staged, At(sum(copies_of[:wanted[-1] + 1]), i, sum(copies_of)).v)

            def stage(s, d, i, tail):
                if s - d >= 0:
                    return None if tail or s - d >= n else (s - d, i)
                if isinstance(i, int) and i == 0:
                    return None
                return (s - d + n, i - 1)

            def run(eng, steps, enter=None, last=0):
                steps(0, range(n), False)
                if times > 1:
                    with eng.Fori(1, times) as i:
                        if enter:
                            dve_step.enter(i, enter)
                        steps(i, range(n), False)
                        if enter:
                            dve_step.leave(1, times)
                steps(times, range(last), True)

            def y_of(u):
                return ys.index(u) if u in ys else None

            DEPTH = 8 + lag

            def pe_part(pe):
                def steps(i, ss, tail):
                    for s in ss:
                        if (x := stage(s, 0, i, tail)) is not None:
                            u, it = x
                            wait_staged(pe, 0, u, it)
                            wait_free(pe, logits_ready, u, 2, it)
                            parts = units[u]["scores"]
                            for j, (q, k) in enumerate(parts):
                                ins = pe.matmul(PS[u % 2][:, 0:nk(u)], q, k, start=j == 0,
                                                stop=j == len(parts) - 1)
                            ins.then_inc(scores_ready, 1)
                        if (x := stage(s, 2, i, tail)) is not None:
                            u, it = x
                            pe.wait_ge(probs_ready, count(u, it).v)
                            wait_free(pe, turned_copied, u, 2, it)
                            pe.wait_ge(const_loaded, CONST_DMAS)
                            for at_k, rows in kts(u):
                                ins = pe.transpose(PT[u % 2][0:rows, at_k:at_k + P],
                                                   LP(u)[:, at_k:at_k + rows], ident[:, :])
                            ins.then_inc(turned_ready, 1)
                        if (x := stage(s, 4, i, tail)) is not None:
                            u, it = x
                            pe.wait_ge(turned_copied, count(u, it).v)
                            wait_free(pe, out_used, u, 2, it)
                            pe.wait_ge(const_loaded, CONST_DMAS)
                            for b, (at_k, rows) in enumerate(kts(u)):
                                ins = pe.matmul(PO[u % 2][:, 0:units[u]["vd"]],
                                                PTs(u)[0:rows, at_k:at_k + P], units[u]["v"](b, it),
                                                start=b == 0, stop=b == len(kts(u)) - 1)
                            ins.then_inc(out_ready, 1)
                        if (x := stage(s, 6 + lag, i, tail)) is not None and y_of(x[0]) is not None:
                            k, it = y_of(x[0]), x[1]
                            pe.wait_ge(y_ready, count(k, it, ny).v)
                            wait_free(pe, y_lo, k, 2, it, ny)
                            pe.transpose(pg[k % 2][:, 0:P], y(k), ident[:, :]).then_inc(y_turned, 1)

                run(pe, steps, last=DEPTH)

            def act_part(act):
                def steps(i, ss, tail):
                    for s in ss:
                        if (x := stage(s, 2, i, tail)) is not None:
                            u, it = x
                            rows = min(P, nk(u))
                            act.wait_ge(turned_ready, count(u, it).v)
                            wait_free(act, out_ready, u, 2, it)
                            act.activation(PTs(u)[0:rows, 0:len(kts(u)) * P],
                                           PT[u % 2][0:rows, 0:len(kts(u)) * P],
                                           ACT.Copy).then_inc(turned_copied, 1)
                        if (x := stage(s, 0, i, tail)) is not None:
                            u, it = x
                            act.wait_ge(logits_ready, count(u, it).v)
                            act.activation(LP(u)[:, 0:nk(u)], LP(u)[:, 0:nk(u)], ACT.Exp, scale=-1.0,
                                           bias=col(0, u), accum_out=col(1, u)).then_inc(probs_ready, 1)
                        if (x := stage(s, 6 + lag, i, tail)) is not None and y_of(x[0]) is not None:
                            k, it = y_of(x[0]), x[1]
                            c = units[ys[k]]["i"] * P
                            act.wait_ge(y_turned, count(k, it, ny).v)
                            act.activation(FH[:, at["tile"](k, it), c:c + P], pg[k % 2][:, 0:P], ACT.Copy,
                                           scale=gain).then_inc(y_hi, 1)

                run(act, steps, last=DEPTH)

            def dve_part(dve):
                names = dict(col=col, ycol=ycol, count=count, wait_free=wait_free, out_ready=out_ready,
                             out_used=out_used, weights_ready=weights_ready, y_turned=y_turned, y_ready=y_ready,
                             y_summed=y_summed, probs_ready=probs_ready, ny=ny, junk=junk, n=n,
                             wait_staged=wait_staged)

                def steps(i, ss, tail):
                    for s in ss:
                        if (x := stage(s, 0, i, tail)) is not None:
                            u, it = x
                            wait_staged(dve, 1, u, it)
                            dve.wait_ge(scores_ready, count(u, it).v)
                            wait_free(dve, turned_ready, u, 4, it)
                            dve.memset(small[:, 150 + u % 6:151 + u % 6], 0.0)
                            dve.tensor_tensor_reduce(LP(u)[:, 0:nk(u)], PS[u % 2][:, 0:nk(u)],
                                                     units[u]["bias"], -units[u]["scale"], 3.0e38,
                                                     ALU.add, ALU.min, col(0, u)).then_inc(logits_ready, 1)
                        if normed_out and (x := stage(s, 8, i, tail)) is not None and y_of(x[0]) is not None:
                            k, it = y_of(x[0]), x[1]
                            dve.wait_ge(y_rstd, count(k, it, ny).v)
                            dve.tensor_scalar(y(k), y(k), ycol(1, k), None, ALU.mult).then_inc(y_ready, 1)
                        if (x := stage(s, 5, i, tail)) is not None:
                            u, it = x
                            k = min(j for j in range(ny) if ys[j] >= u)
                            at["finish"](dve, u, it, k, y(k), PO[u % 2][:, 0:units[u]["vd"]], names)
                        if (x := stage(s, 2, i, tail)) is not None:
                            u, it = x
                            at["weight"](dve, u, it, names)
                        if (x := stage(s, 7 + lag, i, tail)) is not None and y_of(x[0]) is not None:
                            k, it = y_of(x[0]), x[1]
                            c = units[ys[k]]["i"] * P
                            tile = at["tile"](k, it)
                            dve.wait_ge(y_hi, count(k, it, ny).v)
                            dve.scalar_tensor_tensor(FL[:, tile, c:c + P], pg[k % 2][:, 0:P], gain,
                                                     FH[:, tile, c:c + P].bitcast(F32), ALU.mult,
                                                     ALU.subtract).then_inc(y_lo, 1)

                run(dve, steps, enter=at["steps"], last=DEPTH)

            def pool_part(pool):
                def stage_group(i, g):
                    group = groups[g]
                    freed = (scores_ready, logits_ready, weights_ready)[group["reader"]]
                    wait_free(pool, freed, group["last"] - n, 0, i)
                    pool.wait_ge(const_loaded, CONST_DMAS)
                    if "after" in group and isinstance(i, int) and i == 0:
                        pool.wait_ge(*group["after"])
                    for dst, src, *rows in group["copies"](i):
                        if rows:
                            mask = head_rows(rows[0]).broadcast_to([P, dst.shape[-1]])
                            ins = pool.tensor_tensor(dst, src, mask, ALU.mult)
                        else:
                            ins = pool.tensor_copy(dst, src)
                        ins.then_inc(staged, 1)

                def steps(i, ss, tail):
                    first = isinstance(i, int) and i == 0
                    for g in [] if tail else first_order if first else range(len(groups)):
                        stage_group(i, g)

                if not normed_out:
                    run(pool, steps)
                    return

                def both(i, ss, tail, more=True):
                    first = isinstance(i, int) and i == 0
                    for s in ss:
                        for g, group in enumerate(groups):
                            if tail:
                                break
                            if first and s == 0:
                                stage_group(0, g)
                            elif group["last"] + 2 == s and more:
                                stage_group(i + 1, g)
                            elif group["last"] + 2 == s + n and not first:
                                stage_group(i, g)
                        if (x := stage(s, 6, i, tail)) is not None and y_of(x[0]) is not None:
                            k, it = y_of(x[0]), x[1]
                            pool.wait_ge(y_summed, count(k, it, ny).v)
                            pool.tensor_tensor(ycol(1, k), ycol(0, k), cst[:, 3:4], ALU.pow)\
                                .then_inc(y_rstd, 1)

                both(0, range(n), False)
                with pool.Fori(1, times - 1) as i:
                    both(i, range(n), False)
                both(times - 1, range(n), False, more=False)
                both(times, range(DEPTH), True)

            return dict(pe=pe_part, act=act_part, dve=dve_part, pool=pool_part,
                        y=(y_lo, times * ny))

        def weight_plain(dve, u, i, s):
            dve.wait_ge(s["probs_ready"], s["count"](u, i).v)
            dve.reciprocal(s["col"](2, u), s["col"](1, u)).then_inc(s["weights_ready"], 1)

        def finish_plain(units):
            def finish(dve, u, i, k, y, O, s):
                unit = units[u]
                dve.wait_ge(s["out_ready"], s["count"](u, i).v)
                dve.wait_ge(s["weights_ready"], s["count"](u, i).v)
                if unit["first"]:
                    s["wait_free"](dve, s["y_turned"], k, YR, i, s["ny"])
                c = unit["cols"]
                ins = dve.tensor_scalar(y[:, c:c + unit["vd"]], O, s["col"](2, u), None, ALU.mult)
                ins.then_inc(s["out_used"], 1)
                if unit.get("last"):
                    dve.engine_nop().then_inc(s["y_ready"], 1)
            return finish

        def weight_sparse(units):
            def weight(dve, u, i, s):
                unit, col = units[u], s["col"]
                s["wait_staged"](dve, 2, u, i)
                dve.wait_ge(s["probs_ready"], s["count"](u, i).v)
                g = SC[:, 15, 248 + 6 * unit["i"] + unit["gate"]:249 + 6 * unit["i"] + unit["gate"]]
                rows = cst[:, 2:3] if unit["br"] == 0 and unit["i"] == 0 else 1.0
                dve_then(dve, dve.reciprocal(col(2, u), col(1, u)))
                dve.tensor_scalar(col(3, u), col(2, u), g, rows, ALU.mult, ALU.mult)\
                    .then_inc(s["weights_ready"], 1)
            return weight

        def finish_sparse(units):
            def finish(dve, u, i, k, y, O, s):
                unit, col = units[u], s["col"]
                dve.wait_ge(s["out_ready"], s["count"](u, i).v)
                dve.wait_ge(s["weights_ready"], s["count"](u, i).v)
                if unit["first"]:
                    s["wait_free"](dve, s["y_turned"], k, YR, i, s["ny"])
                c = unit["cols"]
                if unit["br"] == 0:
                    ins = dve.tensor_scalar(y[:, c:c + HD], O, col(3, u), None, ALU.mult)
                else:
                    dve.wait_ge(s["out_used"], s["count"](u - 1, i).v)
                    ins = dve.scalar_tensor_tensor(y[:, c:c + HD], O, col(3, u), y[:, c:c + HD],
                                                   ALU.mult, ALU.add)
                ins.then_inc(s["out_used"], 1)
                if unit.get("last"):
                    dve.engine_nop().then_inc(s["y_ready"], 1)
            return finish

        def weight_diff(units):
            def weight(dve, u, i, s):
                col = s["col"]
                dve.wait_ge(s["probs_ready"], s["count"](u, i).v)
                if units[u]["first"]:
                    dve.reciprocal(col(2, u), col(1, u)).then_inc(s["weights_ready"], 1)
                else:
                    dve_then(dve, dve.reciprocal(col(3, u), col(1, u)))
                    dve.tensor_scalar(col(2, u), col(3, u), lamt[:, 1:2], None, ALU.mult)\
                        .then_inc(s["weights_ready"], 1)
            return weight

        def finish_diff(units):
            def finish(dve, u, i, k, y, O, s):
                unit, col = units[u], s["col"]
                dve.wait_ge(s["out_ready"], s["count"](u, i).v)
                dve.wait_ge(s["weights_ready"], s["count"](u, i).v)
                if unit["first"]:
                    s["wait_free"](dve, s["y_turned"], k, YR, i, s["ny"])
                    dve.tensor_scalar(y, O, col(2, u), None, ALU.mult).then_inc(s["out_used"], 1)
                else:
                    dve.wait_ge(s["out_used"], s["count"](u - 1, i).v)
                    dve.scalar_tensor_tensor(y, O, col(2, u), y, ALU.mult, ALU.add)\
                        .then_inc(s["out_used"], 1)
                    dve.wait_ge(s["out_used"], s["count"](u, i).v)
                    dve.tensor_tensor_reduce(s["junk"](k), y, y, 1.0 / P, RMS_EPS, ALU.mult, ALU.add,
                                             s["ycol"](0, k)).then_inc(s["y_summed"], 1)
            return finish


        def mem_attention(l, slot):
            units = []
            for pair in range(2):
                for i in range(QT):
                    for hh in range(2):
                        units.append(dict(
                            i=i, nk=MEM, vd=HD, cols=hh * HD, first=hh == 0, last=hh == 1, scale=HD ** -0.5,
                            bias=SC[:, 15, 0:MEM],
                            scores=[(SC[:, 2 * pair + hh, i * P:(i + 1) * P], mem_k[:, l, pair, :])],
                            v=lambda b, it, pair=pair, hh=hh: mem_v[:, l, b, pair * P + hh * HD:
                                                                   pair * P + (hh + 1) * HD]))
            return attention(dict(
                name=f"mem{l}", units=units, times=1, LP=5, steps=0,
                tile=lambda k, it: 6 + k // QT, finish=finish_plain(units), weight=weight_plain,
                groups=[dict(reader=0, need=8 * pair, last=8 * pair + 7, copies=lambda it, pair=pair: [
                    (SC[:, 2 * pair + hh, :], arena[:, slot + pair, :], hh) for hh in range(2)])
                    for pair in range(2)]))

        def sparse_attention():
            units = []
            for i in reversed(range(QT)):
                for g in range(2):
                    for br in range(BR):
                        nk = NC_ if br == 0 else (i + 1) * P
                        key = [kc[:, 0:NC_], arena[:, KS, 0:nk], arena[:, KW, 0:nk]][br]
                        bias = SC[:, 15, 62 * i + 31 * g:62 * i + 31 * g + 31] if br == 0 else \
                            SC[:, 7 + g, (QT - 1 - i) * P:S]
                        v = (lambda b, it, g=g: vc[0:NC_, g, :]) if br == 0 else \
                            (lambda b, it, g=g, br=br: arena[:, VSW + b // 2, (b % 2) * CW + (br - 1) * P
                                                             + g * HD:(b % 2) * CW + (br - 1) * P + (g + 1) * HD])
                        units.append(dict(i=i, br=br, nk=nk, vd=HD, cols=g * HD, gate=3 * g + br,
                                          first=(g, br) == (0, 0), last=(g, br) == (1, 2), scale=1.0,
                                          bias=bias, scores=[(SC[:, 5 * g, i * P:(i + 1) * P], key)], v=v))
            per_i = 2 * BR
            groups = []
            for b in range(QT):
                i, u = QT - 1 - b, per_i * b
                cols = slice(b * P, (b + 1) * P)
                groups += [
                    dict(reader=0, need=u, last=u + per_i - 1, copies=lambda it, i=i: [
                        (SC[:, 5 * g, i * P:(i + 1) * P], arena[:, bass.ds(it + QN, 1), i * P:(i + 1) * P], g)
                        for g in range(2)]),
                    dict(reader=1, need=u, last=u + BR, after=(ev_used, BASE["bias_c"]["T"] + 12),
                         copies=lambda it, i=i: [
                        (compressed(g)[:, i:i + 1], CMPB[:, i:i + 1, bass.ds(it * NC_ + 6 * g * NC_, NC_)])
                        for g in range(2)]),
                    dict(reader=2, need=u, last=u + per_i - 1, copies=lambda it, i=i: [
                        (gate_cols(g)[:, i:i + 1], gates[:, i:i + 1, bass.ds(it * BR + 18 * g, BR)])
                        for g in range(2)])]
                groups += [dict(reader=1, need=1 + BR * g, last=u + per_i - 1 - BR * (1 - g),
                                copies=lambda it, g=g, cols=cols: [
                    (SC[:, 7 + g, cols], arena[:, bass.ds(it + BIAS_E + 6 * g, 1), cols])]) for g in range(2)]
            compressed = lambda g: SC[:, 15, 0:248].rearrange("p (i g c) -> p i g c", i=QT, g=2)[:, :, g, :]
            gate_cols = lambda g: SC[:, 15, 248:272].rearrange("p (i g c) -> p i g c", i=QT, g=2)[:, :, g, :]
            return attention(dict(
                name="sparse", units=units, times=6, LP=1, steps=len(units),
                tile=lambda k, it: bass.ds(it, 1), finish=finish_sparse(units),
                weight=weight_sparse(units),
                groups=groups))

        def mla_attention():
            units = []
            for hh in range(2):
                for i in range(QT):
                    nk, q = (i + 1) * P, slice(i * P, (i + 1) * P)
                    units.append(dict(
                        i=i, nk=nk, vd=P, cols=0, first=True, last=True, hh=hh, scale=MLA_SCALE,
                        bias=sq[:, 0, (QT - 1 - i) * P:S],
                        scores=[(SC[:, hh, q], SC[:, 3 + hh, 0:nk]),
                                (SC[:, 2 + 7 * hh, q], SC[:, 15, 0:nk])],
                        v=lambda b, it, hh=hh: V_MLA[:, b, bass.ds(it * 2 * P + hh * P, P)]))
            return attention(dict(
                name="latent", units=units, times=4, LP=5, steps=0,
                tile=lambda k, it: bass.ds(it * 2 + k // QT, 1), finish=finish_plain(units),
                weight=weight_plain,
                groups=[dict(reader=0, need=4 * hh, last=4 * hh + 3, copies=lambda it, hh=hh: [
                    (SC[:, hh, :], arena[:, bass.ds(it * 2 + hh, 1), :]),
                    (SC[:, 2 + 7 * hh, :], SC[:, bass.ds(it + 11, 1), :], hh),
                    (SC[:, 3 + hh, :], arena[:, bass.ds(it * 2 + 8 + hh, 1), :])]) for hh in range(2)]))

        def diff_attention():
            QD = ((0, 1), (2, 9))
            units = []
            for hh in range(2):
                for i in range(QT):
                    for m in range(2):
                        nk = (i + 1) * P
                        units.append(dict(
                            i=i, nk=nk, vd=P, cols=0, first=m == 0, last=m == 1, scale=DIFF_SCALE,
                            bias=sq[:, 0, (QT - 1 - i) * P:S],
                            scores=[(SC[:, QD[hh][m], i * P:(i + 1) * P], SC[:, 3 + hh, 0:nk])],
                            v=lambda b, it, hh=hh: V_DIFF[:, b, bass.ds(it * 2 * P + hh * P, P)]))
            return attention(dict(
                name="diff", units=units, times=4, LP=5, steps=len(units) // 2,
                tile=lambda k, it: bass.ds(it * 2 + k // QT, 1), finish=finish_diff(units), norm=True,
                weight=weight_diff(units), gain=gainB("sub"),
                groups=[dict(reader=0, need=8 * hh, last=8 * hh + 7, copies=lambda it, hh=hh: [
                    (SC[:, QD[hh][m], :], arena[:, bass.ds(it * 2 + hh, 1), :], m) for m in range(2)] + [
                    (SC[:, 3 + hh, :], arena[:, bass.ds(it * 2 + 8 + hh, 1), :])]) for hh in range(2)]))

        CMPB = SC[:, 9:12, :].rearrange("p a n -> p (a n)")[:, 0:QT * NH * NC_]\
            .rearrange("p (i c) -> p i c", i=QT)
        att = [mem_attention(0, QMEM0), sparse_attention(), mem_attention(1, QMEM1), mla_attention(),
               diff_attention()]
        MIXED = {"out0": [0], "out1": [1, 2], "out2": [3], "out3": [4]}

        def mixed_ready(pe, name):
            if name == "out0":
                pe.wait_ge(operand_ready, BASE["out0"]["M"])
            for k in MIXED[name]:
                pe.wait_ge(*att[k]["y"])

        cols_of = lambda w, c0, n=CW: kpn(w)[:, :, c0:c0 + n]

        block = ctx.enter_context(nc.Block())

        @block.sync
        def _(sp):
            xin = SF[:, 0:8, :].rearrange("p (q a) n -> p q (a n)", q=QT)
            mem_in = SF[:, 8:12, :].rearrange("p (q a) n -> p q (a n)", q=2)
            sp.dma_start(xin, a["x"][0].rearrange("(q p) d -> p q d", p=P)).then_inc(input_loaded, 16)
            sp.dma_start(mem_in, a["mem"][0].rearrange("(q p) d -> p q d", p=P)).then_inc(mem_loaded, 16)

            vec = lambda v: v.rearrange("(k p) -> k p", p=P)

            def rows(dst, src):
                sp.dma_start(dst, src).then_inc(rows_loaded, 16)
                sent[0] += 16

            sent = [0]
            rowB = lambda name, k, n, c0=0, c1=P: SC[COL_B[name] + k:COL_B[name] + k + n, 1, c0:c1]
            rows(rowB("conv", 0, 18), a["a_conv_w"][0].rearrange("k (c p) -> (k c) p", p=P))
            rows(rowB("qn", 0, 3), vec(a["mla_q_norm_2"][0]))
            rows(rowB("kn", 0, 2), vec(a["mla_kv_norm_2"][0]))
            rows(rowB("sub", 0, 1), vec(a["diff_subln_2"][0]))
            for h in range(2):
                for name, n, v in (("bq", 1, a["b_q_gain"]), ("kg", 3, a["k_gain"]),
                                   ("mq", 2, a["mem_q_gain"]), ("mk", 2, a["mem_k_gain"])):
                    rows(rowB(name, 0, n, h * HD, (h + 1) * HD), v)
            rows(rowB("pos", 0, 32), a["cmp_pos"].rearrange("v (t two) d -> (v t) (two d)", two=2))
            assert sent[0] == ROW_DMAS_B

            def stream(name, parts):
                for c, p in enumerate(parts):
                    load_chunk(sp, At(BASE[name]["C"] + c), p)

            def stream_out(name, w):
                stream(name, [[(full(CW), cols_of(w, c * CW))] for c in range(4)])

            def stream_mlp(name, up, down):
                up_q = up.rearrange("(k p) n -> p k n", p=P)
                down_q = down.rearrange("(q k p) n -> p q k n", p=P, q=FQ)
                with sp.Fori(0, FQ) as i:
                    for j in range(8):
                        src = up_q[:, :, bass.ds(i * D + j * CW, CW)] if j < 4 else \
                            down_q[:, bass.ds(i, 1), :, (j - 4) * CW:(j - 3) * CW]
                        load_chunk(sp, At(BASE[name]["C"] + j, i, 8), [(full(CW), src)])

            mk = a["mem_w_kv"]
            stream("mem", [[(full(CW), cols_of(mk[l], c * CW))] for l in range(2) for c in range(2)])
            stream("a_in", [[(full(CW), cols_of(a["a_w_in"][0], part * CONV + pr * CW))]
                            for pr in range(3) for part in range(3)] +
                   [[(full(CW), cols_of(a["a_w_in"][0], 3 * CONV))]])
            stream_out("out0", a["w_out"][0])
            stream_mlp("mlp0", a["w_up"][0], a["w_down"][0])
            wkv = a["w_kv_shared"]
            pair = lambda o: (lambda r: full(CW)(r)[:, :, o:o + P])
            stream("kv", [[(full(CW), cols_of(wkv, 0))]] +
                   [[(pair(0), cols_of(wkv, c0, P)), (pair(P), cols_of(wkv, c0 + 2 * P, P))]
                    for c0 in (2 * P, 3 * P)])
            stream("cmp", [[(full(CW), kpn(a["cmp_w1"][kv])[:, h * KT:(h + 1) * KT, :])]
                           for kv in range(2) for h in range(2)])
            wb = a["b_w_in"][0]
            spread = lambda t, g: (lambda r: full(CW)(r)[:, :, t * P + g * HD:t * P + (g + 1) * HD])
            stream("b_in", [[(spread(t, g), cols_of(wb, (g * 6 + 2 * c + t) * HD, HD))
                             for t in range(2) for g in range(2)] for c in range(3)] +
                   [[(full(36), cols_of(wb, CONV, 36))], [(full(CW), cols_of(wb, CONV + 36))]])
            wo = a["w_out"][1]
            part_rows = lambda g: (lambda r: full(CW)(r)[g * HD:(g + 1) * HD, 0:6, :])
            stream("out1", [[(part_rows(g), wo[g * 6 * HD:(g + 1) * 6 * HD, c * CW:(c + 1) * CW]
                              .rearrange("(t d) n -> d t n", d=HD)) for g in range(2)] +
                            [(lambda r: full(CW)(r)[:, 6:8, :],
                              wo[CONV:D, c * CW:(c + 1) * CW].rearrange("(k p) n -> p k n", p=P))]
                            for c in range(4)])
            stream_mlp("mlp1", a["w_up"][1], a["w_down"][1])
            dq, dkv = a["mla_w_dq_2"][0], a["mla_w_dkv_2"][0]
            halfcols = lambda o: (lambda r: full(P)(r)[:, :, o * HD:(o + 1) * HD])
            stream("mla_a", [[(full(CW), cols_of(dq, 0))], [(full(P), cols_of(dq, CW, P))],
                             [(full(CW), cols_of(dkv, 0))],
                             [(halfcols(o), cols_of(dkv, CW, HD)) for o in range(2)]])
            uq = kpn(a["mla_w_uq_2"][0]).rearrange("p k (h n) -> p k h n", n=192)
            ukv = kpn(a["mla_w_ukv_2"][0]).rearrange("p k (h n) -> p k h n", n=256)
            heads = lambda k, h, n: (lambda r: r[:, k * h * n:(k + 1) * h * n]
                                     .rearrange("p (h n) -> p h n", h=h))
            stream("mla_b", [[(heads(k, 4, P), uq[:, k, 4 * c:4 * c + 4, 0:P]) for k in range(3)]
                             for c in range(2)] +
                   [[(heads(k, 8, HD), uq[:, k, :, P:192]) for k in range(3)],
                    [(heads(k, 8, P), ukv[:, k, :, 0:P]) for k in range(2)],
                    [(heads(k, 8, P), ukv[:, k, :, P:256]) for k in range(2)]])
            stream_out("out2", a["mla_w_o_2"][0])
            stream_mlp("mlp2", a["ffn_w_up_2"][0], a["ffn_w_down_2"][0])
            stream("diff", [[(full(CW), cols_of(a["diff_w_qkv_2"][0], c * CW))] for c in range(12)])
            stream_out("out3", a["diff_w_o_2"][0])
            stream_mlp("mlp3", a["ffn_w_up_2"][1], a["ffn_w_down_2"][1])
            out = a["out"][0].rearrange("(q p) (h n) -> p q h n", p=P, h=2)
            for k in range(8):
                sp.wait_ge(ev_used, BASE["turn_out"]["T"] + k + 1)
                sp.dma_start(out[:, k // 2, k % 2, :], SC[:, k, :]).then_inc(stored, 16)
            sp.wait_ge(stored, 16 * 8)

        @block.gpsimd
        def _(pool):
            sent = [0]

            def const(dst, src):
                pool.dma_start(dst, src).then_inc(const_loaded, 16)
                sent[0] += 16

            const(halves[:, :], a["c_halves"])
            const(cst[:, :], a["c_cols"])
            const(arena[0:33, 12:16, :], a["c_onehot"].rearrange("b (s n) -> b s n", s=4))
            const(arena[0:32, 16, 0:NH], a["rel_bias"])
            const(arena[32:33, 16, 0:NH], a["c_neg"])
            for j, name in enumerate(("q1", "k1", "q2", "k2")):
                v = a[f"diff_lambda_{name}_2"]
                const(lam_in[:, j, :], bass.AP(v.tensor, v.offset, [[0, P], [1, HD]]))
            const(w2s[:, :, :, :], a["cmp_w2"].rearrange("v (j p) d -> p v j d", p=P))
            assert sent[0] == CONST_DMAS

            pool.dma_start(perm[:, :], a["c_flip"]).then_inc(perm_loaded, 16)
            pool.wait_ge(ev_used, BASE["bias_v"]["T"] + 4)
            pool.dma_start(vec_rows.rearrange("h (s n) -> h s n", s=4), SF[0:NH, 12:16, :])\
                .then_inc(bias_stored, 16)
            pool.wait_ge(bias_stored, 16)
            pool.wait_ge(acc_ready, BASE["mem"]["T"])
            hank = bass.AP(vec_rows.tensor, vec_rows.offset, [[1, P], [2048, NH], [1, S]])
            pool.dma_start(arena[:, BIAS_E:BIAS_E + NH, :], hank).then_inc(hankel_loaded, 16)
            pool.wait_ge(ev_used, BASE["out0"]["T"])
            att[0]["pool"](pool)
            pool.wait_ge(acc_ready, BASE["cmp"]["T"] + 2)
            for hh in range(4):
                src = bass.AP(vec_rows.tensor, vec_rows.offset + hh * 2048 + 1025,
                              [[CSTR, NC_], [4 * 2048, 3], [1, S]])
                pool.dma_start(SF[hh * NC_:(hh + 1) * NC_, 8:11, :], src).then_inc(cmp_rows_loaded, 16)
            pool.dma_start(perm[:, :], a["c_keys"]).then_inc(perm_loaded, 16)
            pool.wait_ge(ev_used, BASE["b_in"]["T"] + 10)
            att[1]["pool"](pool)
            pool.wait_ge(*att[1]["y"])
            att[2]["pool"](pool)
            pool.wait_ge(*att[2]["y"])
            pos = bass.AP(a["positions_2"].tensor, a["positions_2"].offset, [[0, P], [1, S]])
            pool.dma_start(W_MLA[:, 2, :].bitcast(I32), pos).then_inc(pos_loaded, 16)
            pool.dma_start(perm[:, :], a["c_rope_latent"]).then_inc(perm_loaded, 16)
            scale_pool(pool, "split2")
            pool.wait_ge(ev_used, BASE["mla_b"]["T"] + 1)
            pool.dma_start(sq[:, 0, :], a["c_mask"]).then_inc(mask_loaded, 16)
            pool.wait_ge(rotated, 1)
            att[3]["pool"](pool)
            pool.dma_start(perm[:, :], a["c_rope_diff"]).then_inc(perm_loaded, 16)
            scale_pool(pool, "ln2a", "lmb0")
            scale_pool(pool, "ln2b", "lfb0")
            pool.wait_ge(acc_ready, BASE["diff"]["T"])
            pool.dma_start(SF[:, 2, :].bitcast(I32), pos).then_inc(pos_loaded, 16)
            pool.wait_ge(ev_used, BASE["diff"]["T"] + 1)
            pool.dma_start(sq[:, 0, :], a["c_mask"]).then_inc(mask_loaded, 16)
            pool.wait_ge(ev_used, BASE["diff"]["T"] + 38)
            att[4]["pool"](pool)
            scale_pool(pool, "ln3a", "lmb1")

        @block.tensor
        def _(pe):
            xin = SF[:, 0:8, :].rearrange("p (q a) n -> p q (a n)", q=QT)
            mem_in = SF[:, 8:12, :].rearrange("p (q a) n -> p q (a n)", q=2)
            pe.wait_ge(ident_loaded, 16)
            pe.wait_ge(eps_set, 1)
            pe.wait_ge(input_loaded, 16)
            turn_pe(pe, "turn_x", KT, lambda k: [xin[:, q, k * P:(k + 1) * P] for q in range(QT)], P)
            pe.wait_ge(mem_loaded, 16)
            turn_pe(pe, "turn_mem", KT, lambda k: [mem_in[:, q, k * P:(k + 1) * P] for q in range(2)], P,
                    after=lambda: stats(pe, BASE["turn_x"]["R"], BASE["turn_x"]["Q"]))
            pe.wait_ge(long_rows_loaded, ROW_DMAS_A)
            pe.wait_ge(rows_loaded, ROW_DMAS_B)
            t = At(BASE["turn_col"]["T"])
            for n, rows in enumerate((N_A, N_B)):
                pe.transpose(bank_for(pe, t + n)[:, 0:rows], SC[0:rows, n, 0:P], ident[0:rows, 0:rows])\
                    .then_inc(acc_ready, 1)
            pe.wait_ge(const_loaded, CONST_DMAS)
            stats(pe, BASE["turn_mem"]["R"], BASE["turn_mem"]["Q"], N=MEM)
            bias_v_pe(pe)
            turn_rstd(pe, BASE["norm_mem"]["G"], MEM)
            mem_pe(pe)
            pe.wait_ge(perm_loaded, 16)
            turn_rstd(pe, BASE["norm_a"]["G"])
            bias_e_pe(pe)
            a_in_pe(pe)
            att[0]["pe"](pe)
            mixed_ready(pe, "out0")
            out_pe(pe, "out0")
            x_end_pe(pe, "out0")
            turn_rstd(pe, BASE["norm_f0"]["G"])
            mlp_all(pe, "mlp0", mlp_pe)
            turn_rstd(pe, BASE["norm_kv"]["G"])
            kv_pe(pe)
            turn_rstd(pe, BASE["norm_b"]["G"])
            cmp_pe(pe)
            b_in_pe(pe)
            bias_c_pe(pe)
            cmp_out_pe(pe)
            pe.wait_ge(ev_used, BASE["cmp_out"]["T"] + 4)
            att[1]["pe"](pe)
            att[2]["pe"](pe)
            mixed_ready(pe, "out1")
            out_pe(pe, "out1")
            x_end_pe(pe, "out1")
            turn_rstd(pe, BASE["norm_f1"]["G"])
            mlp_all(pe, "mlp1", mlp_pe)
            mla_a_pe(pe)
            mla_b_pe(pe)
            mla_v_pe(pe)
            pe.wait_ge(rotated, 1)
            att[3]["pe"](pe)
            mixed_ready(pe, "out2")
            out_pe(pe, "out2")
            ln_pe(pe, "ln2a")
            mlp_all(pe, "mlp2", mlp_pe)
            ln_pe(pe, "ln2b")
            diff_pe(pe)
            pe.wait_ge(rotated, 2)
            att[4]["pe"](pe)
            mixed_ready(pe, "out3")
            out_pe(pe, "out3")
            ln_pe(pe, "ln3a")
            mlp_all(pe, "mlp3", mlp_pe)
            ln_pe(pe, "ln3b")
            pe.wait_ge(x_final, KT)
            turn_pe(pe, "turn_out", 8, lambda k: [X[:, 4 * (k % 2) + j, (k // 2) * P:(k // 2 + 1) * P]
                                                  for j in range(4)], P)

        @block.scalar
        def _(act):
            act.dma_start(ident[:, :], a["c_ident"]).then_inc(ident_loaded, 16)
            row_load = lambda dst, src: act.dma_start(dst, src).then_inc(long_rows_loaded, 16)
            vec = lambda v: v.rearrange("(k p) -> k p", p=P)
            rowA = lambda name, k=8: SC[COL_A[name]:COL_A[name] + k, 0, 0:P]
            vec = lambda v: v.rearrange("(k p) -> k p", p=P)
            for name, v in (("mix0", a["mix_norm"][0]), ("mix1", a["mix_norm"][1]), ("kvn", a["kv_norm"]),
                            ("memn", a["mem_norm"]), ("mlp0", a["mlp_norm"][0]), ("mlp1", a["mlp_norm"][1])):
                row_load(rowA(name), vec(v))
            for tag, key in (("lmg", "ln_mix_g_2"), ("lmb", "ln_mix_b_2"), ("lfg", "ln_ffn_g_2"),
                             ("lfb", "ln_ffn_b_2")):
                row_load(rowA(tag + "0", 16), a[key].rearrange("l (k p) -> (l k) p", p=P))
            act.wait_ge(eps_set, 1)
            for k in range(KT):
                t = BASE["turn_x"]["T"] + k
                evac(act, At(t))
                if k:
                    x_tile_act(act, "turn_x", k - 1, t - 1)
            x_tile_act(act, "turn_x", KT - 1, t)
            memT = arena[:, 0:4, :].rearrange("p a (b n) -> p (a b) n", n=MEM)
            for k in range(KT):
                t = BASE["turn_mem"]["T"] + k
                evac(act, At(t), N=MEM)
                if k == 1:
                    x_end_act(act, "turn_x")
                if k:
                    act.wait_ge(ev_used, t)
                    square(act, BASE["turn_mem"]["Q"] + k - 1, memT[:, k - 1, :], MEM)
            act.wait_ge(ev_used, t + 1)
            square(act, BASE["turn_mem"]["Q"] + KT - 1, memT[:, KT - 1, :], MEM)
            t = At(BASE["turn_col"]["T"])
            evac(act, t, N=N_A)
            evac(act, t + 1, N=N_B)
            split_hi(act, At(0))
            act.wait_ge(const_loaded, CONST_DMAS)
            act.wait_ge(lam_in_ready, 1)
            act.activation(lamt[:, 2:4], lamt[:, 0:2], ACT.Exp).then_inc(lam_exp, 1)
            plain_act(act, "bias_v", 4, rows=NH)
            root(act, BASE["turn_mem"]["R"], D, N=MEM)
            norm_act(act, "norm_mem", HH, MEM)
            mem_act(act)
            norm_act(act, "norm_a", HH, between={k: lambda e, k=k: [
                evac(e, At(BASE["bias_e"]["T"] + h)) for h in (2 * k, 2 * k + 1)] for k in range(NH // 2)})
            a_in_act(act)
            att[0]["act"](act)
            out_act(act, "out0")
            norm_act(act, "norm_f0", HH)
            mlp_all(act, "mlp0", mlp_act)
            norm_act(act, "norm_kv", HH)
            kv_act(act)
            kv_next = BASE["kv"]["C"] + 3
            split_hi(act, At(kv_next + 1))
            norm_act(act, "norm_b", HH, between={0: lambda e: split_hi(e, At(kv_next + 2)),
                                                 3: lambda e: split_hi(e, At(kv_next + 3)),
                                                 6: lambda e: split_hi(e, At(kv_next + 4))})
            cmp_act(act)
            b_in_act(act)
            plain_act(act, "bias_c", 12, N=124)
            cmp_out_act(act)
            att[1]["act"](act)
            att[2]["act"](act)
            out_act(act, "out1")
            norm_act(act, "norm_f1", HH)
            mlp_all(act, "mlp1", mlp_act)
            mla_a_act(act)
            mla_b_act(act)
            mla_v_act(act)
            att[3]["act"](act)
            out_act(act, "out2")
            ln_act(act, "ln2a", "lmb0")
            mlp_all(act, "mlp2", mlp_act)
            ln_act(act, "ln2b", "lfb0")
            diff_act(act)
            att[4]["act"](act)
            out_act(act, "out3")
            ln_act(act, "ln3a", "lmb1")
            mlp_all(act, "mlp3", mlp_act)
            ln_act(act, "ln3b", "lfb1")
            plain_act(act, "turn_out", 8)

        @block.vector
        def _(dve):
            dve_step.add(dve.memset(ones[:, :], 1.0))
            dve_step.add(dve.memset(eps[:, 0:1], RMS_EPS))
            dve.memset(eps[:, 1:2], LN_EPS).then_inc(eps_set, 1)
            dve.wait_ge(dve_step.sem, dve_step.n)
            for k in range(KT):
                t = BASE["turn_x"]["T"] + k
                keep(dve, At(t), X[:, k, :])
                if k:
                    x_tile_dve(dve, "turn_x", k - 1, t - 1)
            x_tile_dve(dve, "turn_x", KT - 1, t)
            memT = arena[:, 0:4, :].rearrange("p a (b n) -> p (a b) n", n=MEM)
            b = BASE["turn_mem"]
            for k in range(KT):
                keep(dve, At(b["T"] + k), memT[:, k, :], N=MEM)
                if k:
                    add_square(dve, b["Q"] + k - 1, b["R"] if k == 1 else None, MEM)
            add_square(dve, b["Q"] + KT - 1, None, MEM)
            t = At(BASE["turn_col"]["T"])
            keep(dve, t, colA[:, :], N=N_A)
            keep(dve, t + 1, colB[:, :], N=N_B)
            dve.wait_ge(ev_used, (t + 2).v)
            dve_then(dve, dve.tensor_scalar(gainB("bq"), gainB("bq"), HD ** -0.5, None, ALU.mult))
            dve_then(dve, dve.tensor_scalar(gainB("sub"), gainB("sub"), 1.0 - LAM0, None, ALU.mult))
            dve.wait_ge(const_loaded, CONST_DMAS)
            dve_then(dve, dve.tensor_tensor_reduce(val[:, 0, 0:HD], lam_in[:, 0, :], lam_in[:, 1, :], 1.0, 0.0,
                                                   ALU.mult, ALU.add, lamt[:, 0:1]))
            dve.tensor_tensor_reduce(val[:, 0, HD:P], lam_in[:, 2, :], lam_in[:, 3, :], 1.0, 0.0,
                                     ALU.mult, ALU.add, lamt[:, 1:2]).then_inc(lam_in_ready, 1)
            dve.wait_ge(lam_exp, 1)
            dve_then(dve, dve.tensor_tensor(lamt[:, 0:1], lamt[:, 3:4], lamt[:, 2:3], ALU.subtract))
            dve_then(dve, dve.tensor_scalar(lamt[:, 1:2], lamt[:, 0:1], -LAM0, None, ALU.add))
            for k in range(4):
                keep(dve, At(BASE["bias_v"]["T"] + k), SF[0:NH, 12 + k, :], rows=NH)
                if k == 1:
                    split_lo(dve, At(0))
            norm_dve(dve, "norm_mem", memT, "memn", BASE["turn_mem"]["R"], MEM)
            mem_dve(dve)
            norm_dve(dve, "norm_a", X, "mix0", BASE["turn_x"]["R"], between={k: lambda e, k=k: [
                keep(e, At(BASE["bias_e"]["T"] + h), arena[:, BIAS_E + h, :]) for h in (2 * k, 2 * k + 1)]
                for k in range(NH // 2)})
            a_in_dve(dve)
            dve.memset(SC[:, 15, 0:MEM], 0.0).then_inc(zeros_set, 1)
            dve.wait_ge(zeros_set, 1)
            att[0]["dve"](dve)
            out_dve(dve, "out0")
            norm_dve(dve, "norm_f0", X, "mlp0", BASE["out0"]["R"])
            mlp_all(dve, "mlp0", mlp_dve)
            norm_dve(dve, "norm_kv", X, "kvn", BASE["mlp0"]["R"])
            kv_dve(dve)
            kv_next = BASE["kv"]["C"] + 3
            split_lo(dve, At(kv_next + 1))
            norm_dve(dve, "norm_b", X, "mix1", BASE["mlp0"]["R"],
                     between={0: lambda e: split_lo(e, At(kv_next + 2)),
                              3: lambda e: split_lo(e, At(kv_next + 3)),
                              6: lambda e: split_lo(e, At(kv_next + 4))})
            cmp_dve(dve)
            b_in_dve(dve)
            plain_dve(dve, "bias_c", 12, lambda n: CMPB[:, n % 4, (n // 4) * 124:(n // 4 + 1) * 124], N=124)
            cmp_out_dve(dve)
            att[1]["dve"](dve)
            dve.memset(SC[:, 15, 0:MEM], 0.0).then_inc(zeros_set, 1)
            dve.wait_ge(zeros_set, 2)
            att[2]["dve"](dve)
            out_dve(dve, "out1")
            norm_dve(dve, "norm_f1", X, "mlp1", BASE["out1"]["R"])
            mlp_all(dve, "mlp1", mlp_dve)
            mla_a_dve(dve)
            mla_b_dve(dve)
            mla_v_dve(dve)
            dve.wait_ge(mask_loaded, 16)
            att[3]["dve"](dve)
            dve.wait_ge(x_scaled, KT)
            out_dve(dve, "out2")
            ln_dve(dve, "ln2a", "lmg0", "lmb0")
            mlp_all(dve, "mlp2", mlp_dve)
            ln_dve(dve, "ln2b", "lfg0", "lfb0")
            diff_dve(dve)
            dve.engine_nop().then_inc(rotated, 1)
            dve.wait_ge(mask_loaded, 32)
            att[4]["dve"](dve)
            dve.wait_ge(x_scaled, 3 * KT)
            out_dve(dve, "out3")
            ln_dve(dve, "ln3a", "lmg1", "lmb1")
            mlp_all(dve, "mlp3", mlp_dve)
            ln_dve(dve, "ln3b", "lfg1", "lfb1")
            plain_dve(dve, "turn_out", 8, lambda k: SC[:, k, :])


CONST_DMAS = 16 * 10
ROW_DMAS_A, ROW_DMAS_B = 16 * (6 + 4), 16 * (4 + 8 + 1)


def bucket(dist):
    n = np.maximum(dist, 0)
    nf = np.maximum(n, 1).astype(np.float32)
    large = 16 + (np.log(nf / np.float32(16)) / np.float32(math.log(1024 / 16)) * np.float32(16)).astype(np.int32)
    return np.where(n < 16, n, np.minimum(large, 31))


def constants():
    p = np.arange(P)
    f = np.float32
    flip = (p[:, None] + p[None, :] == P - 1).astype(f)
    keys = np.zeros((P, P), f)
    for hh in range(4):
        for c in range(NC_):
            keys[hh * NC_ + NC_ - 1 - c, hh * NC_ + c] = 1

    def rotation(block, pairs):
        r = np.zeros((P, P), f)
        for b in range(0, P, block):
            for j in range(pairs):
                r[b + j + pairs, b + j] = -1
                r[b + j, b + j + pairs] = 1
        return r

    dist = np.concatenate([511 - np.arange(1024), np.arange(1024) - 512])
    onehot = np.zeros((33, 2048), f)
    onehot[bucket(dist), np.arange(2048)] = dist >= 0
    onehot[32] = dist < 0
    cols = np.zeros((P, 8), f)
    cols[:, 0] = (10000.0 ** (-2.0 * (p % 32) / 64)).astype(f)
    cols[:, 1] = np.where(p % 64 < 16, 500000.0 ** (-2.0 * (p % 8) / 16), 0).astype(f)
    cols[:, 2] = p >= 31
    cols[:, 3] = -0.5
    cols[:, 4], cols[:, 5] = p < HD, p >= HD
    mask = np.where(384 + p[:, None] - np.arange(S)[None, :] >= 0, 0, NEG).astype(f)
    return dict(c_ident=np.eye(P, dtype=f), c_halves=(p[:, None] // HD == p[None, :] // HD).astype(f),
                c_cols=cols, c_onehot=onehot, c_neg=np.full((1, NH), NEG, f), c_flip=flip, c_keys=keys,
                c_rope_latent=rotation(64, 32), c_rope_diff=rotation(64, 8), c_mask=mask)


def kernel(**inputs):
    from concourse import bacc
    from concourse.bass_utils import run_bass_kernel_spmd

    nc = bacc.Bacc("TRN2", target_bir_lowering=False, num_devices=1)
    arrays, tensors = {}, {}
    for name, v in list(inputs.items()) + list(constants().items()):
        v = np.ascontiguousarray(v)
        arrays[f"in_{name}"] = v
        tensors[name] = nc.dram_tensor(f"in_{name}", v.shape, mybir.dt.from_np(v.dtype),
                                       kind="ExternalInput").ap()
    tensors["out"] = nc.dram_tensor("out_x", (1, S, D), F32, kind="ExternalOutput").ap()
    program(nc, tensors)
    r = run_bass_kernel_spmd(nc, [arrays], core_ids=[0])
    return r.results[0]["out_x"]
```
